# Optimizing a Trainium2 kernel written in Bass

```python
import jax, jax.numpy as jnp
from jax import lax
import numpy as np

D_MODEL = 2048
BATCH = 1
SEQ = 256
DEPTH = 2
DEC_BATCH = 1
DEC_SEQ = 32
PAST_LEN = 128

CHUNK = 64
N_EVEN = (DEPTH + 1) // 2
N_ODD = DEPTH // 2
LRU_WIDTH = D_MODEL // 2
LRU_HEADS = 8
LRU_BLOCK = LRU_WIDTH // LRU_HEADS
CONV_WIDTH = 4
LRU_C = 8.0
MLA_HEADS = 8
QK_NOPE = 128
QK_ROPE = 64
V_DIM = 128
Q_LORA = 512
KV_LORA = 256
ROPE_THETA = 10000.0
Q_BLOCK = 128
IN_COLS = 2 * LRU_WIDTH + Q_LORA + KV_LORA + QK_ROPE
MIX_OUT = LRU_WIDTH + MLA_HEADS * V_DIM
POOL_WINDOWS = (2, 4, 8, 16)
POOL_GROUPS = 4
POOL_GW = D_MODEL // POOL_GROUPS
POOL_BUF = 15
N_MEM = 256
MEM_HEADS = 4
MEM_HEAD_DIM = D_MODEL // MEM_HEADS
D_FF = 4 * D_MODEL
DN_ALPHA = (2.0 * DEPTH) ** 0.25
DN_BETA = (8.0 * DEPTH) ** -0.25
LN_EPS = 1e-5
RMS_EPS = 1e-6

kernel_name = 'hybrid_stream_rglru_mla_pool_step'

F32 = jnp.float32

def layer_norm(x, g, b):
    xf = x.astype(F32)
    mu = jnp.mean(xf, -1, keepdims=True)
    var = jnp.mean(jnp.square(xf - mu), -1, keepdims=True)
    return ((xf - mu) * lax.rsqrt(var + LN_EPS) * g.astype(F32) + b.astype(F32)).astype(x.dtype)

def rms_norm(x, g):
    xf = x.astype(F32)
    return (xf * lax.rsqrt(jnp.mean(jnp.square(xf), -1, keepdims=True) + RMS_EPS) * g.astype(F32)).astype(x.dtype)

def rope(x, pos):
    half = QK_ROPE // 2
    inv = ROPE_THETA ** (-jnp.arange(half, dtype=F32) / half)
    ang = pos.astype(F32)[:, None] * inv[None, :]
    shape = (pos.shape[0],) + (1,) * (x.ndim - 3) + (half,)
    cos, sin = jnp.cos(ang).reshape(shape), jnp.sin(ang).reshape(shape)
    xf = x.astype(F32)
    x1, x2 = xf[..., :half], xf[..., half:]
    return jnp.concatenate([x1 * cos - x2 * sin, x1 * sin + x2 * cos], -1).astype(x.dtype)

def causal_conv(u, buf, w, b):
    full = jnp.concatenate([buf, u], axis=1)
    T = u.shape[1]
    y = b
    for k in range(CONV_WIDTH):
        y = y + w[k] * full[:, k:k + T]
    return y, full[:, full.shape[1] - (CONV_WIDTH - 1):]

def rg_lru(u, h0, ga_w, ga_b, gx_w, gx_b, lam):
    B, T, _ = u.shape
    ub = u.reshape(B, T, LRU_HEADS, LRU_BLOCK)
    r = jax.nn.sigmoid(jnp.einsum('bthi,hij->bthj', ub, ga_w) + ga_b).reshape(B, T, LRU_WIDTH)
    ig = jax.nn.sigmoid(jnp.einsum('bthi,hij->bthj', ub, gx_w) + gx_b).reshape(B, T, LRU_WIDTH)
    log_a = -LRU_C * r.astype(F32) * jax.nn.softplus(-lam.astype(F32))
    a = jnp.exp(log_a)
    bterm = jnp.sqrt(-jnp.expm1(2.0 * log_a)) * (ig * u).astype(F32)
    bterm = bterm.at[:, 0].add(a[:, 0] * h0.astype(F32))

    def combine(left, right):
        a1, b1 = left
        a2, b2 = right
        return a1 * a2, a2 * b1 + b2

    _, h = lax.associative_scan(combine, (a, bterm), axis=1)
    return h.astype(u.dtype), h[:, -1].astype(u.dtype)

def mla_attention(q_nope, q_pe, ckv, kpe, q_pos, w_uk, w_uv):
    B, Tq = q_nope.shape[:2]
    q_lat = jnp.einsum('bqhn,chn->bqhc', q_nope, w_uk)
    scale = (QK_NOPE + QK_ROPE) ** -0.5
    k_chunk = jnp.arange(ckv.shape[1]) // CHUNK

    def block(args):
        ql, qp, qpos = args
        s = jnp.einsum('bqhc,bkc->bhqk', ql, ckv) + jnp.einsum('bqhr,bkr->bhqk', qp, kpe)
        s = s.astype(F32) * scale
        mask = k_chunk[None, :] <= (qpos // CHUNK)[:, None]
        s = jnp.where(mask[None, None], s, -jnp.inf)
        p = jax.nn.softmax(s, axis=-1).astype(ckv.dtype)
        return jnp.einsum('bhqk,bkc->bqhc', p, ckv)

    if Tq > Q_BLOCK and Tq % Q_BLOCK == 0:
        nb = Tq // Q_BLOCK
        split = lambda t: jnp.moveaxis(t.reshape((B, nb, Q_BLOCK) + t.shape[2:]), 1, 0)
        o = lax.map(block, (split(q_lat), split(q_pe), q_pos.reshape(nb, Q_BLOCK)))
        o_lat = jnp.moveaxis(o, 0, 1).reshape(B, Tq, MLA_HEADS, KV_LORA)
    else:
        o_lat = block((q_lat, q_pe, q_pos))
    return jnp.einsum('bqhc,chv->bqhv', o_lat, w_uv).reshape(B, Tq, MLA_HEADS * V_DIM)

def rec_attn_mixer(x, pos, conv_buf, h0, ckv_past, kpe_past,
                   w_in, q_norm_g, w_uq, kv_norm_g, w_uk, w_uv,
                   conv_w, conv_b, ga_w, ga_b, gx_w, gx_b, lam, w_out):
    B, T, _ = x.shape
    z = x @ w_in
    o1 = LRU_WIDTH
    o2 = o1 + LRU_WIDTH
    o3 = o2 + Q_LORA
    o4 = o3 + KV_LORA
    u, gate, c_q, c_kv, k_pe = z[..., :o1], z[..., o1:o2], z[..., o2:o3], z[..., o3:o4], z[..., o4:]
    u_c, new_conv = causal_conv(u, conv_buf, conv_w, conv_b)
    h, h_last = rg_lru(u_c, h0, ga_w, ga_b, gx_w, gx_b, lam)
    rec_out = h * jax.nn.gelu(gate)
    q = (rms_norm(c_q, q_norm_g) @ w_uq).reshape(B, T, MLA_HEADS, QK_NOPE + QK_ROPE)
    q_nope, q_pe = q[..., :QK_NOPE], rope(q[..., QK_NOPE:], pos)
    ckv_new = rms_norm(c_kv, kv_norm_g)
    kpe_new = rope(k_pe, pos)
    ckv_all = jnp.concatenate([ckv_past, ckv_new], axis=1)
    kpe_all = jnp.concatenate([kpe_past, kpe_new], axis=1)
    attn_out = mla_attention(q_nope, q_pe, ckv_all, kpe_all, pos, w_uk, w_uv)
    out = jnp.concatenate([rec_out, attn_out], axis=-1) @ w_out
    return out, new_conv, h_last, ckv_new, kpe_new

def pool_mixer(x, pos, pool_buf, pool_w, pool_scale):
    B, T, D = x.shape
    full_x = jnp.concatenate([pool_buf, x], axis=1)
    full = full_x.astype(F32)
    cs = jnp.concatenate([jnp.zeros((B, 1, D), F32), jnp.cumsum(full, axis=1)], axis=1)
    end = cs[:, POOL_BUF + 1:]
    outs = []
    for g, w in enumerate(POOL_WINDOWS):
        sl = slice(g * POOL_GW, (g + 1) * POOL_GW)
        start = cs[:, POOL_BUF + 1 - w:POOL_BUF + 1 - w + T, sl]
        cnt = jnp.minimum(pos + 1, w).astype(F32)[None, :, None]
        outs.append((end[..., sl] - start) / cnt - full[:, POOL_BUF:, sl])
    d = jnp.stack(outs, axis=2).astype(x.dtype)
    y = jnp.einsum('btgi,gij->btgj', d, pool_w).reshape(B, T, D) * pool_scale
    return y, full_x[:, full_x.shape[1] - POOL_BUF:]

def cross_attention(x, mem_k, mem_v, wq, wo):
    B, T, _ = x.shape
    q = (x @ wq).reshape(B, T, MEM_HEADS, MEM_HEAD_DIM)
    k = mem_k.reshape(B, -1, MEM_HEADS, MEM_HEAD_DIM)
    v = mem_v.reshape(B, -1, MEM_HEADS, MEM_HEAD_DIM)
    s = jnp.einsum('bqhd,bkhd->bhqk', q, k).astype(F32) * (MEM_HEAD_DIM ** -0.5)
    p = jax.nn.softmax(s, axis=-1).astype(x.dtype)
    o = jnp.einsum('bhqk,bkhd->bqhd', p, v).reshape(B, T, D_MODEL)
    return o @ wo

def sq_relu_mlp(x, w_up, w_down):
    return jnp.square(jax.nn.relu(x @ w_up)) @ w_down

def trunk(x, t_past, mem_k, mem_v, conv_buf, h0, ckv_past, kpe_past, pool_buf, W):
    T = x.shape[1]
    pos = t_past + jnp.arange(T)
    convs, hs, ckvs, kpes, pools = [], [], [], [], []
    for l in range(DEPTH):
        j = l // 2
        if l % 2 == 0:
            mix, c, hh, ck, kp = rec_attn_mixer(
                x, pos, conv_buf[j], h0[j], ckv_past[j], kpe_past[j],
                W['w_in'][j], W['q_norm_g'][j], W['w_uq'][j], W['kv_norm_g'][j], W['w_uk'][j], W['w_uv'][j],
                W['conv_w'][j], W['conv_b'][j], W['gate_a_w'][j], W['gate_a_b'][j],
                W['gate_x_w'][j], W['gate_x_b'][j], W['lru_lambda'][j], W['w_out'][j])
            convs.append(c); hs.append(hh); ckvs.append(ck); kpes.append(kp)
        else:
            mix, pb = pool_mixer(x, pos, pool_buf[j], W['pool_w'][j], W['pool_scale'][j])
            pools.append(pb)
        x = layer_norm(DN_ALPHA * x + mix, W['ln_g'][l, 0], W['ln_b'][l, 0])
        x = layer_norm(DN_ALPHA * x + cross_attention(x, mem_k[l], mem_v[l], W['xa_wq'][l], W['xa_wo'][l]),
                       W['ln_g'][l, 1], W['ln_b'][l, 1])
        x = layer_norm(DN_ALPHA * x + sq_relu_mlp(x, W['mlp_up'][l], W['mlp_down'][l]),
                       W['ln_g'][l, 2], W['ln_b'][l, 2])
    return x, jnp.stack(convs), jnp.stack(hs), jnp.stack(ckvs), jnp.stack(kpes), jnp.stack(pools)

def setup_inputs(seed: int = 0) -> dict:
    key = jax.random.key(seed)
    ks = iter(jax.random.split(key, 40))
    nrm = lambda shape, scale: scale * jax.random.normal(next(ks), shape, F32)
    u = jax.random.uniform(next(ks), (N_EVEN, LRU_WIDTH), F32, 0.9, 0.999)
    s = u ** (1.0 / LRU_C)
    lru_lambda = jnp.log(s) - jnp.log1p(-s)
    return {
        'x_prompt': nrm((BATCH, SEQ, D_MODEL), 1.0),
        'x_sample': nrm((DEC_BATCH, DEC_SEQ, D_MODEL), 1.0),
        'mem_prompt': nrm((BATCH, N_MEM, D_MODEL), 1.0),
        'cache_mem_k': nrm((DEPTH, DEC_BATCH, N_MEM, D_MODEL), 1.0),
        'cache_mem_v': nrm((DEPTH, DEC_BATCH, N_MEM, D_MODEL), 1.0),
        'cache_mla_ckv': nrm((N_EVEN, DEC_BATCH, PAST_LEN, KV_LORA), 1.0),
        'cache_mla_kpe': nrm((N_EVEN, DEC_BATCH, PAST_LEN, QK_ROPE), 1.0),
        'state_rglru_h': nrm((N_EVEN, DEC_BATCH, LRU_WIDTH), 1.0),
        'state_rglru_conv': nrm((N_EVEN, DEC_BATCH, CONV_WIDTH - 1, LRU_WIDTH), 1.0),
        'state_pool': nrm((N_ODD, DEC_BATCH, POOL_BUF, D_MODEL), 1.0),
        'w_in': nrm((N_EVEN, D_MODEL, IN_COLS), D_MODEL ** -0.5),
        'q_norm_g': 1.0 + nrm((N_EVEN, Q_LORA), 0.02),
        'w_uq': nrm((N_EVEN, Q_LORA, MLA_HEADS * (QK_NOPE + QK_ROPE)), Q_LORA ** -0.5),
        'kv_norm_g': 1.0 + nrm((N_EVEN, KV_LORA), 0.02),
        'w_uk': nrm((N_EVEN, KV_LORA, MLA_HEADS, QK_NOPE), KV_LORA ** -0.5),
        'w_uv': nrm((N_EVEN, KV_LORA, MLA_HEADS, V_DIM), KV_LORA ** -0.5),
        'conv_w': nrm((N_EVEN, CONV_WIDTH, LRU_WIDTH), CONV_WIDTH ** -0.5),
        'conv_b': nrm((N_EVEN, LRU_WIDTH), 0.01),
        'gate_a_w': nrm((N_EVEN, LRU_HEADS, LRU_BLOCK, LRU_BLOCK), LRU_BLOCK ** -0.5),
        'gate_a_b': nrm((N_EVEN, LRU_HEADS, LRU_BLOCK), 0.01),
        'gate_x_w': nrm((N_EVEN, LRU_HEADS, LRU_BLOCK, LRU_BLOCK), LRU_BLOCK ** -0.5),
        'gate_x_b': nrm((N_EVEN, LRU_HEADS, LRU_BLOCK), 0.01),
        'lru_lambda': lru_lambda,
        'w_out': nrm((N_EVEN, MIX_OUT, D_MODEL), DN_BETA * MIX_OUT ** -0.5),
        'pool_w': nrm((N_ODD, POOL_GROUPS, POOL_GW, POOL_GW), DN_BETA * POOL_GW ** -0.5),
        'pool_scale': 1.0 + nrm((N_ODD, D_MODEL), 0.1),
        'xa_wq': nrm((DEPTH, D_MODEL, D_MODEL), D_MODEL ** -0.5),
        'xa_wk': nrm((DEPTH, D_MODEL, D_MODEL), D_MODEL ** -0.5),
        'xa_wv': nrm((DEPTH, D_MODEL, D_MODEL), D_MODEL ** -0.5),
        'xa_wo': nrm((DEPTH, D_MODEL, D_MODEL), DN_BETA * D_MODEL ** -0.5),
        'mlp_up': nrm((DEPTH, D_MODEL, D_FF), D_MODEL ** -0.5),
        'mlp_down': nrm((DEPTH, D_FF, D_MODEL), DN_BETA * D_FF ** -0.5),
        'ln_g': 1.0 + nrm((DEPTH, 3, D_MODEL), 0.02),
        'ln_b': nrm((DEPTH, 3, D_MODEL), 0.02),
    }

def reference(x_prompt, x_sample, mem_prompt, cache_mem_k, cache_mem_v, cache_mla_ckv, cache_mla_kpe,
              state_rglru_h, state_rglru_conv, state_pool,
              w_in, q_norm_g, w_uq, kv_norm_g, w_uk, w_uv, conv_w, conv_b,
              gate_a_w, gate_a_b, gate_x_w, gate_x_b, lru_lambda, w_out,
              pool_w, pool_scale, xa_wq, xa_wk, xa_wv, xa_wo, mlp_up, mlp_down, ln_g, ln_b):
    W = dict(w_in=w_in, q_norm_g=q_norm_g, w_uq=w_uq, kv_norm_g=kv_norm_g, w_uk=w_uk, w_uv=w_uv,
             conv_w=conv_w, conv_b=conv_b, gate_a_w=gate_a_w, gate_a_b=gate_a_b,
             gate_x_w=gate_x_w, gate_x_b=gate_x_b, lru_lambda=lru_lambda, w_out=w_out,
             pool_w=pool_w, pool_scale=pool_scale, xa_wq=xa_wq, xa_wo=xa_wo,
             mlp_up=mlp_up, mlp_down=mlp_down, ln_g=ln_g, ln_b=ln_b)
    bp = x_prompt.shape[0]
    dt = x_prompt.dtype
    p_mem_k = jnp.einsum('bmd,lde->lbme', mem_prompt, xa_wk)
    p_mem_v = jnp.einsum('bmd,lde->lbme', mem_prompt, xa_wv)
    y_prompt, p_conv, p_h, p_ckv, p_kpe, p_pool = trunk(
        x_prompt, 0, p_mem_k, p_mem_v,
        jnp.zeros((N_EVEN, bp, CONV_WIDTH - 1, LRU_WIDTH), dt),
        jnp.zeros((N_EVEN, bp, LRU_WIDTH), dt),
        jnp.zeros((N_EVEN, bp, 0, KV_LORA), dt),
        jnp.zeros((N_EVEN, bp, 0, QK_ROPE), dt),
        jnp.zeros((N_ODD, bp, POOL_BUF, D_MODEL), dt), W)
    y_sample, s_conv, s_h, s_ckv, s_kpe, s_pool = trunk(
        x_sample, cache_mla_ckv.shape[2], cache_mem_k, cache_mem_v,
        state_rglru_conv, state_rglru_h, cache_mla_ckv, cache_mla_kpe, state_pool, W)
    return (y_prompt, y_sample, p_conv, p_h, p_ckv, p_kpe, p_pool, p_mem_k, p_mem_v,
            s_conv, s_h, s_ckv, s_kpe, s_pool)


_drawn_inputs = setup_inputs


def setup_inputs(seed=0):
    import zlib

    import numpy as np

    out = dict(_drawn_inputs(seed))
    spreads = {}
    factors = {'cache_mla_kpe': 3.662,
     'q_norm_g': 8.0,
     'kv_norm_g': 2.925,
     'gate_a_b': 23.676,
     'gate_x_b': 8.0}
    for name, (base, spread) in spreads.items():
        noise = np.random.default_rng([zlib.crc32(name.encode()), seed]).standard_normal(out[name].shape)
        drawn = base * np.exp(spread * noise) if base else spread * noise
        out[name] = __import__('jax').numpy.asarray(drawn.astype(out[name].dtype))
    for name, factor in factors.items():
        out[name] = (out[name] * factor).astype(out[name].dtype)
    return out
```

```python
from contextlib import ExitStack

import numpy as np
import concourse.bass as bass
from concourse import mybir

D, TP, TS, T = 2048, 256, 32, 288
P = 128
NK = D // P
DEPTH, NMEM, FF, PAST = 2, 256, 8192, 128
LW, LT = 1024, 8
QL, KVL, ROPE, HEADS = 512, 256, 64, 8
IN_COLS = 2 * LW + QL + KVL + ROPE
KEYS = TP + PAST + TS
ALPHA = (2.0 * DEPTH) ** 0.25
LN_EPS, RMS_EPS = 1e-5, 1e-6
MLA_SCALE = (128 + ROPE) ** -0.5
XA_SCALE = 512 ** -0.5
WINDOWS = (2, 4, 8, 16)
PBUF = 15
UW = 3 + TP + 3 + TS
CW = UW - 3
EW = 2 * PBUF + T
CHUNK_ELEMS = 2048
RAW_SLOTS, SPLIT_SLOTS = 4, 2

C_ID, C_PERM, C_COS, C_SIN = 0, 128, 256, 256 + T
C_MASK = C_SIN + T
C_CNT = C_MASK + 512
C_END = C_CNT + 64


def build(nc, a, o):
    f32, f32r = mybir.dt.float32, mybir.dt.float32r
    ALU, ACT, AX = mybir.AluOpType, mybir.ActivationFunctionType, mybir.AxisListType
    ds = bass.ds

    KB = 1024
    lay, total = {}, 0

    def place(name, nbytes):
        nonlocal total
        lay[name] = total
        total += -(-nbytes // 32) * 32

    for name, nbytes in (("X", 18 * KB), ("XH", 18 * KB), ("XL", 18 * KB), ("RAW", 32 * KB), ("WH", 16 * KB),
                         ("WL", 16 * KB), ("AREA", 72 * KB), ("CST", C_END * 4), ("PR", 310 * 4), ("ONES", 512),
                         ("RS", T * 4), ("RELU", 2 * T * 4), ("SQH", 2 * 2 * T * 4), ("SMALL", 1600)):
        place(name, nbytes)
    base = -(-nc.sbuf_base // 32) * 32
    nc.alloc_sbuf_tensor("arena", [P, (total + 64) // 4], f32)
    at_area = lay["AREA"]

    def sb(name, shape, where, dt=f32):
        return nc.alloc_sbuf_tensor_at(name, shape, dt, offset=base + where)

    def area(name, shape, off, dt=f32):
        n = 4
        for s in shape[1:]:
            n *= s
        assert off % 32 == 0 and off + n <= 72 * KB, name
        return sb(name, shape, at_area + off, dt)

    X = sb("X", [P, NK, T], lay["X"])
    XH = sb("XH", [P, NK, T], lay["XH"], f32r)
    XL = sb("XL", [P, NK, T], lay["XL"], f32r)
    RAW = sb("RAW", [P, RAW_SLOTS, CHUNK_ELEMS], lay["RAW"])
    WH = sb("WH", [P, SPLIT_SLOTS, CHUNK_ELEMS], lay["WH"], f32r)
    WL = sb("WL", [P, SPLIT_SLOTS, CHUNK_ELEMS], lay["WL"], f32r)
    CST = sb("CST", [P, C_END], lay["CST"])
    PR = sb("PR", [P, 310], lay["PR"])
    ONES = sb("ONES", [P, P], lay["ONES"])
    RS = sb("RS", [P, T], lay["RS"])
    RELU = sb("RELU", [P, 2, T], lay["RELU"])
    SQH = sb("SQH", [P, 2, 2, T], lay["SQH"])
    SMALL = sb("SMALL", [P, 400], lay["SMALL"])

    ID, PERM = CST[:, C_ID:C_ID + P], CST[:, C_PERM:C_PERM + P]
    COS, SIN = CST[:, C_COS:C_COS + T], CST[:, C_SIN:C_SIN + T]
    MASK = CST[:, C_MASK:C_MASK + 512]
    R0 = 192
    LNG = lambda l, s, k: PR[:, (l * 3 + s) * NK + k:(l * 3 + s) * NK + k + 1]
    LNB = lambda l, s, k: PR[:, 96 + (l * 3 + s) * NK + k:96 + (l * 3 + s) * NK + k + 1]
    col = lambda c: PR[:, R0 + c:R0 + c + 1]
    P_CONVW, P_CONVB, P_GAB, P_GXB, P_LAM, P_H0, P_CST, P_PSC, P_QN, P_KN = 0, 32, 40, 48, 56, 64, 72, 96, 112, 116

    XIN = area("XIN", [P, 3, D], 0)
    MIN = area("MIN", [P, 2, D], 24 * KB)
    STG = area("STG", [P, 2, 1024], 24 * KB)
    PN = sb("PN", [P, 3, P], lay["XL"])
    MTH = area("MTH", [P, NK, NMEM], 40 * KB, f32r)
    MTL = area("MTL", [P, NK, NMEM], 56 * KB, f32r)
    UE = area("UE", [P, LT, UW], 0)
    TT = area("TT", [P, LT, CW], 0)
    UC = area("UC", [P, LT, CW + 1], 9408)
    GT = area("GT", [P, LT, T], 18752)
    RR = area("RR", [P, LT, CW + 1], 27968)
    IG = area("IG", [P, LT, CW + 1], 37312)
    GW = area("GW", [P, 2 * LT, P], 46656)
    QN = area("QN", [P, HEADS, T], 0)
    QP = area("QP", [P, HEADS // 2, T], 9216)
    KN = area("KN", [P, HEADS, KEYS], 13824)
    VV = area("VV", [P, 4, 1024], 27136)
    CQH = area("CQH", [P, 4, T], 27136, f32r)
    CQL = area("CQL", [P, 4, T], 31744, f32r)
    CKT = area("CKT", [P, 2, 512], 43520)
    CKH = area("CKH", [P, 2, 512], 47616, f32r)
    CKL = area("CKL", [P, 2, 512], 51712, f32r)
    KP = area("KP", [P, KEYS], 55808)
    CPN = area("CPN", [P, KVL + 2 * ROPE], 57472 + 32)
    CQ = area("CQ", [P, 4, T], 61056)
    CKV = area("CKV", [P, 2, T], 65664)
    KPE = area("KPE", [P, T], 67968)
    SQM = area("SQM", [P, 4, T], 69120)
    SM = [area(f"SM{n}", [P, 512], 61056 + 2048 * n) for n in range(2)]
    PT = [area(f"PT{n}", [P, 512], 61056 + 4096 + 2048 * n) for n in range(2)]
    OST = area("OST", [P, 3, 320], 69248 - 0)
    SQ = area("SQ", [P, NK, T], 0)
    QX = area("QX", [P, NK, T], 0)
    KNAT = [area(f"KNAT{n}", [P, 4, 512], 18432 + 8192 * n) for n in range(2)]
    VS = area("VS", [P, 2, D], 18432)
    VP = [area(f"VP{n}", [P, 2, 512], 34816 + 4096 * n) for n in range(2)]
    KT = [area(f"KT{n}", [P, 4, 512], 43008 + 8192 * n) for n in range(2)]
    SX = [area(f"SX{n}", [P, 512], 59392 + 2048 * n) for n in range(2)]
    PX = [area(f"PX{n}", [P, 512], 63488 + 2048 * n) for n in range(2)]
    HH = area("HH", [P, 32, T], 0, f32r)
    HL = area("HL", [P, 32, T], 36 * KB, f32r)
    EXT = area("EXT", [P, NK, EW], 0)
    S2 = area("S2", [P, NK, EW], 20352)
    S4 = area("S4", [P, 12, EW], 40704)
    S8 = area("S8", [P, 8, EW], 55968)
    S16 = area("S16", [P, 4, EW], 66144)
    SPN = area("SPN", [P, D], 40704)
    PST = area("PST", [P, 2, D], 20352)
    YST = area("YST", [P, 3, D], 18432)

    ps = nc.alloc_psum_tensor("ps", [P, 8, 512], f32)
    S = {}

    KINDS = {
        "ln": (["ln00", "ln01", "ln02", "ln10", "ln11", "ln12"],
               dict(d=4, sq=4, var=1, eps=1, root=1, rs=1, high=NK, low=4, t=NK, x=NK)),
        "xa": (["xa0", "xa1"], dict(kin0=64, kin1=64, ktT=16, kt=16, s=4, sm=5, max=5, exp=5, p=5, t=5, pt=5, o=5,
                                    oh=5, ol=5, vin0=32, vin1=32, vs=16)),
        "wq": (["wq0", "wq1"], dict(out0=4, out1=4)),
        "wo": (["wo0", "wo1"], dict(out0=4, out1=4, sum=1)),
        "up": (["upa0", "upb0", "upa1", "upb1"], dict(out0=8, out1=8, high0=8, high1=8, low0=8, low1=8)),
        "down": (["downa0", "downb0", "downa1", "downb1"], dict(out0=4, out1=4, sum=1)),
    }
    NOT_SIGNALLED = {("ln02", "high"), ("ln02", "low"), ("ln12", "high"), ("ln12", "low"), ("downa0", "sum"),
                     ("downa1", "sum")}
    KIND_OF = {n: kind for kind, (names, _) in KINDS.items() for n in names}

    def sem(name):
        which, _, what = name.rpartition("_")
        if which in KIND_OF:
            name = f"{KIND_OF[which]}_{what}"
        if name not in S:
            S[name] = nc.alloc_semaphore(name)
        return S[name]

    def reached(name, n):
        which, _, what = name.rpartition("_")
        before = 0
        if which in KIND_OF:
            names, per = KINDS[KIND_OF[which]]
            before = sum(per[what] for w in names[:names.index(which)] if (w, what) not in NOT_SIGNALLED)
        return sem(name), n + before

    PHASES, c = {}, 0
    for name, n in ([("mem0", 32), ("mem1", 32), ("u", 8), ("gate", 8), ("cq", 4), ("ckv", 2), ("kpe", 1),
                     ("uq", 4), ("uk", 1), ("uv", 1), ("wout", 16)]
                    + [(f"{p}0", n) for p, n in (("wq", 16), ("wo", 16), ("upa", 32), ("downa", 32), ("upb", 32),
                                                 ("downb", 32))]
                    + [("pool", 4)]
                    + [(f"{p}1", n) for p, n in (("wq", 16), ("wo", 16), ("upa", 32), ("downa", 32), ("upb", 32),
                                                 ("downb", 32))]):
        PHASES[name] = c
        c += n
    CHUNKS = c
    load_sem = [sem(f"chunk_loaded{s}") for s in range(RAW_SLOTS)]
    split_hi, chunk_split, chunk_used = sem("chunk_high"), sem("chunk_split"), sem("chunk_used")

    def kt_view(w):
        return w.rearrange("(k p) n -> p k n", p=P)

    def product(out, wh, wl, xh, xl, start, stop):
        nc.tensor.matmul(out, wh, xh, start=start, stop=False)
        nc.tensor.matmul(out, wh, xl, start=False, stop=False)
        return nc.tensor.matmul(out, wl, xh, start=False, stop=stop)

    win = kt_view(a["w_in"][0])
    stack = ExitStack()
    block = stack.enter_context(nc.Block())

    @block.sync
    def _(sp):
        def load(c0, j, step, i, src, fresh=False):
            s, n = (c0 + j) % RAW_SLOTS, (c0 + j) // RAW_SLOTS
            if not fresh:
                sp.wait_ge(chunk_split, c0 + j - RAW_SLOTS + 1 + step * i)
            shape = src.shape
            dst = RAW[:, s, 0:int(np.prod(shape[1:]))].rearrange("p (k n) -> p k n", k=shape[1])
            sp.dma_start(dst, src).then_inc(load_sem[s], 16)

        def mem_body(l, i, fresh=False):
            for half, w in enumerate((a["xa_wk"], a["xa_wv"])):
                for q in range(4):
                    j = 4 * half + q
                    load(PHASES[f"mem{l}"], j, 8, i, kt_view(w[l])[:, 4 * q:4 * q + 4, ds(i * 512, 512)],
                         fresh and j < RAW_SLOTS)

        def linear(name, w, n, col0=0):
            with sp.Fori(0, n) as i:
                for j in range(4):
                    load(PHASES[name], j, 4, i,
                         w[:, 8 * (j % 2):8 * (j % 2) + 8, ds(i * 512 + (col0 + 256 * (j // 2)), 256)])

        def down(name, w):
            with sp.Fori(0, 4) as i:
                for j in range(8):
                    q = j % 4
                    load(PHASES[name], j, 8, i, w[:, 8 * q:8 * q + 8, ds(i * 512 + 256 * (j // 4), 256)])

        mem_body(0, 0, True)
        with sp.Fori(1, 4) as i:
            mem_body(0, i)
        with sp.Fori(0, 4) as i:
            mem_body(1, i)
        linear("u", win, 2)
        linear("gate", win, 2, LW)
        for j in range(4):
            load(PHASES["cq"], j, 0, 0, win[:, 8 * (j % 2):8 * (j % 2) + 8, 2 * LW + 256 * (j // 2):][:, :, 0:256])
        for j in range(2):
            load(PHASES["ckv"], j, 0, 0, win[:, 8 * j:8 * j + 8, 2 * LW + QL:2 * LW + QL + KVL])
        def load_parts(c, srcs, dsts):
            sp.wait_ge(chunk_split, c - RAW_SLOTS + 1)
            for dst, src in zip(dsts, srcs):
                sp.dma_start(dst, src).then_inc(load_sem[c % RAW_SLOTS], 16)

        c0 = PHASES["kpe"]
        twice = RAW[:, c0 % RAW_SLOTS, :].rearrange("p (k h n) -> p k h n", h=2, n=ROPE)
        load_parts(c0, [win[:, :, IN_COLS - ROPE:IN_COLS]] * 2, [twice[:, :, h, :] for h in range(2)])
        for j in range(4):
            c0 = PHASES["uq"] + j
            heads = kt_view(a["w_uq"][0])[:, :, 384 * j:384 * j + 384].rearrange("p k (h n) -> p k h n", h=2)
            slot = RAW[:, c0 % RAW_SLOTS, 0:4 * 384].rearrange("p (k n) -> p k n", k=4)
            load_parts(c0, [heads[:, :, h, part] for h in range(2) for part in (slice(0, P), slice(P, 192))],
                       [slot[:, :, at:at + n] for at, n in ((0, P), (256, ROPE), (P, P), (256 + ROPE, ROPE))])
        load(PHASES["uk"], 0, 0, 0, a["w_uk"][0].rearrange("(k p) h n -> p k (h n)", p=P))
        load(PHASES["uv"], 0, 0, 0, a["w_uv"][0].rearrange("(k p) h n -> p k (h n)", p=P))
        linear("wout", kt_view(a["w_out"][0]), 4)
        for l in range(DEPTH):
            if l == 1:
                for g in range(4):
                    load(PHASES["pool"], g, 0, 0, kt_view(a["pool_w"][0][g]))
            linear(f"wq{l}", kt_view(a["xa_wq"][l]), 4)
            linear(f"wo{l}", kt_view(a["xa_wo"][l]), 4)
            for half, (up, dn) in enumerate((("upa", "downa"), ("upb", "downb"))):
                linear(f"{up}{l}", kt_view(a["mlp_up"][l]), 8, half * FF // 2)
                down(f"{dn}{l}", kt_view(a["mlp_down"][l])[:, 32 * half:32 * half + 32, :])

    GATHERED = {PHASES["kpe"]: 2} | {PHASES["uq"] + n: 4 for n in range(4)}

    def loaded_count(c):
        more = sum(n - 1 for g, n in GATHERED.items() if g <= c and g % RAW_SLOTS == c % RAW_SLOTS)
        return 16 * (c // RAW_SLOTS + 1 + more)

    MLA_UNITS = [("p", h) for h in range(HEADS)] + [("s", g) for g in range(2)]

    @block.tensor
    def _(pe):
        def mem_tiles():
            pe.wait_ge(sem("mem_in"), 32)
            pe.wait_ge(sem("cst_in"), 16)
            for r in range(8):
                b = 4 + r % 4
                if r >= 4:
                    pe.wait_ge(sem("memT_low"), r - 3)
                for k in range(2):
                    for t in range(2):
                        last = nc.tensor.transpose(ps[:, b, k * 256 + t * 128:k * 256 + t * 128 + 128],
                                                   MIN[:, t, (2 * r + k) * P:(2 * r + k + 1) * P], ID)
                last.then_inc(sem("memT"), 1)
            pe.wait_ge(sem("par_in"), 16 * 12)
            pe.wait_ge(sem("memT_low"), 8)
            for t, rows in enumerate((96, 96, 118)):
                last = nc.tensor.transpose(ps[:, 4, t * 128:t * 128 + rows], PN[0:rows, t, :], ID[0:rows, 0:rows])
            last.then_inc(sem("parT"), 1)

        def x_tiles():
            pe.wait_ge(sem("x_in"), 48)
            pe.wait_ge(sem("par_done"), 1)
            for k in range(NK):
                b = 4 + k % 4
                if k >= 4:
                    pe.wait_ge(sem("xT_low"), k - 3)
                for t, rows in enumerate((128, 128, 32)):
                    last = nc.tensor.transpose(ps[:, b, t * 128:t * 128 + rows],
                                               XIN[0:rows, t, k * P:(k + 1) * P], ID[0:rows, 0:rows])
                last.then_inc(sem("xT"), 1)

        def mem_body(l, i):
            c0 = PHASES[f"mem{l}"]
            for half in range(2):
                pe.wait_ge(sem(f"mem_out{half}"), i + 4 * l)
                for q in range(4):
                    j = 4 * half + q
                    h = (c0 + j) % SPLIT_SLOTS
                    pe.wait_ge(chunk_split, c0 + j + 1 + 8 * i)
                    for k in range(4):
                        kk = 4 * q + k
                        for t in range(2):
                            last = product_moving(ps[:, 2 * half + t, :], kk, t, WH[:, h, k * 512:k * 512 + 512],
                                                  WL[:, h, k * 512:k * 512 + 512], kk == 0, kk == NK - 1)
                    last.then_inc(chunk_used, 1)

        def product_moving(out, kk, t, wh, wl, start, stop):
            mh, ml = MTH[:, kk, t * P:(t + 1) * P], MTL[:, kk, t * P:(t + 1) * P]
            nc.tensor.matmul(out, mh, wh, start=start, stop=False)
            nc.tensor.matmul(out, mh, wl, start=False, stop=False)
            return nc.tensor.matmul(out, ml, wh, start=False, stop=stop)

        def chunk_mms(h, bank, rhs, first, last_, ready=None):
            for k in range(8):
                for m in range(2):
                    w = slice(k * 256 + m * P, k * 256 + m * P + P)
                    xh, xl = rhs(k)
                    mm = product(ps[:, bank + m, 0:T], WH[:, h, w], WL[:, h, w], xh, xl,
                                 first and k == 0, last_ and k == 7)
            return mm

        def linear_body(name, i, ln=None, sums=None, blocks=2, before=None):
            c0 = PHASES[name]
            for b in range(blocks):
                if before:
                    pe.wait_ge(sem(f"{before[0]}{b}"), before[1])
                pe.wait_ge(*reached(f"{name}_out{b}", i))
                for q in range(2):
                    j = 2 * b + q
                    if ln is not None:
                        pe.wait_ge(*reached(f"{ln}_low", 2 * (q + 1)))
                    pe.wait_ge(chunk_split, c0 + j + 1 + 4 * i)
                    chunk_mms((c0 + j) % SPLIT_SLOTS, 2 * b,
                              lambda k: (XH[:, 8 * q + k, :], XL[:, 8 * q + k, :]), q == 0, q == 1
                              ).then_inc(chunk_used, 1)
                    if j == 0 and sums:
                        sums(i)

        def sum_tiles(name, b0, first, stop_at):
            def emit(i):
                pe.wait_ge(*reached(f"{name}_out0", i))
                pe.wait_ge(*reached(f"{name}_out1", i))
                for t in range(4):
                    tile = X[:, ds(i * 4 - 4 + t, 1), :].rearrange("p o n -> p (o n)")
                    nc.tensor.matmul(ps[:, 4, 0:T], ONES[:, :], tile, start=False, stop=False,
                                     skip_group_check=True)
            return emit

        def static_sums(name, tiles, start, stop):
            for n, t in enumerate(tiles):
                last = nc.tensor.matmul(ps[:, 4, 0:T], ONES[:, :], X[:, t, :], start=start and n == 0,
                                        stop=stop and n == len(tiles) - 1, skip_group_check=True)
            return last

        def residual_linear(name, body, n):
            body(0, None)
            body_sum0 = static_first(name)
            body(1, body_sum0)
            with pe.Fori(2, n) as i:
                body(i, sum_tiles(name, None, None, None))
            pe.wait_ge(*reached(f"{name}_out0", n))
            pe.wait_ge(*reached(f"{name}_out1", n))
            static_sums(name, range(4 * n - 4, 4 * n), False, True).then_inc(sem(f"{name}_sum"), 1)

        def static_first(name):
            def emit(i):
                pe.wait_ge(*reached(f"{name}_out0", 1))
                pe.wait_ge(*reached(f"{name}_out1", 1))
                static_sums(name, range(4), True, False)
            return emit

        def variance(ln):
            for q in range(4):
                pe.wait_ge(*reached(f"{ln}_sq", q + 1))
                for k in range(4):
                    last = nc.tensor.matmul(ps[:, 5, 0:T], ONES[:, :], SQ[:, 4 * q + k, :],
                                            start=q == 0 and k == 0, stop=q == 3 and k == 3)
            last.then_inc(sem(f"{ln}_var"), 1)

        def down_body(name, i, sums=None):
            c0 = PHASES[name]
            for b in range(2):
                pe.wait_ge(*reached(f"{name}_out{b}", i))
                for q in range(4):
                    j = 4 * b + q
                    pe.wait_ge(chunk_split, c0 + j + 1 + 8 * i)
                    chunk_mms((c0 + j) % SPLIT_SLOTS, 2 * b,
                              lambda k: (HH[:, 8 * q + k, :], HL[:, 8 * q + k, :]), q == 0, q == 3
                              ).then_inc(chunk_used, 1)
                    if j == 0 and sums:
                        sums(i)

        mem_tiles()
        x_tiles()
        pe.wait_ge(sem("memT_low"), 8)
        for l in range(2):
            with pe.Fori(0, 4) as i:
                mem_body(l, i)

        pe.wait_ge(sem("xT_low"), NK)
        with pe.Fori(0, 2) as i:
            linear_body("u", i, before=("mem_out", 8))
        with pe.Fori(0, 2) as i:
            linear_body("gate", i, before=("u_out", 2))
        pe.wait_ge(sem("gates_in"), 32)
        pe.wait_ge(sem("conv"), 4 * LT)
        for n in range(2 * LT):
            if n >= 4:
                pe.wait_ge(sem("gates_sig"), n - 3)
            nc.tensor.matmul(ps[:, 4 + n % 4, 0:CW], GW[:, n, :], UC[:, n % LT, 0:CW], start=True,
                             stop=True).then_inc(sem("gate_mm"), 1)
        linear_body("cq", 0, before=("gate_out", 2))
        c0 = PHASES["ckv"]
        pe.wait_ge(sem("cq_out0"), 1)
        for q in range(2):
            pe.wait_ge(chunk_split, c0 + q + 1)
            chunk_mms((c0 + q) % SPLIT_SLOTS, 0, lambda k: (XH[:, 8 * q + k, :], XL[:, 8 * q + k, :]),
                      q == 0, q == 1).then_inc(chunk_used, 1)
        c0 = PHASES["kpe"]
        pe.wait_ge(sem("cq_out1"), 1)
        pe.wait_ge(chunk_split, c0 + 1)
        for k in range(NK):
            w = slice(k * P, (k + 1) * P)
            last = product(ps[:, 2, 0:T], WH[:, c0 % SPLIT_SLOTS, w], WL[:, c0 % SPLIT_SLOTS, w], XH[:, k, :],
                           XL[:, k, :], k == 0, k == NK - 1)
        last.then_inc(chunk_used, 1)

        pe.wait_ge(sem("gates_sig"), 2 * LT)
        pe.wait_ge(sem("sq_q"), 1)
        for k in range(4):
            last = nc.tensor.matmul(ps[:, 4, 0:T], ONES[:, :], SQM[:, k, :], start=k == 0, stop=k == 3)
        last.then_inc(sem("ssum"), 1)
        pe.wait_ge(sem("sq_kv"), 1)
        for k in range(2):
            last = nc.tensor.matmul(ps[:, 5, 0:T], ONES[:, :], SQM[:, k, :], start=k == 0, stop=k == 1)
        last.then_inc(sem("ssum"), 1)
        pe.wait_ge(sem("past_in"), 48)
        for n in range(3):
            last = nc.tensor.transpose(ps[:, 6, n * P:(n + 1) * P], CPN[:, n * P:(n + 1) * P], ID)
        last.then_inc(sem("pastT"), 1)
        pe.wait_ge(sem("state_cols"), 4)
        nc.tensor.transpose(ps[0:64, 7, 0:P], SMALL[:, 0:64], ID).then_inc(sem("stateT"), 1)

        c0 = PHASES["uq"]
        pe.wait_ge(sem("cq_low"), 1)
        for n in range(4):
            h = (c0 + n) % SPLIT_SLOTS
            pe.wait_ge(chunk_split, c0 + n + 1)
            if n >= 1:
                pe.wait_ge(sem("q_out"), n)
            for m in range(3):
                for k in range(4):
                    w = slice(k * 384 + m * P, k * 384 + m * P + P)
                    last = product(ps[:, m, 0:T], WH[:, h, w], WL[:, h, w], CQH[:, k, :], CQL[:, k, :],
                                   k == 0, k == 3)
            last.then_inc(chunk_used, 1)
        pe.wait_ge(sem("q_out"), 4)
        pe.wait_ge(sem("stateT_out"), 1)
        pe.wait_ge(sem("pastT_out"), 2)
        pe.wait_ge(sem("rms"), 2)
        for n in range(4):
            last = nc.tensor.matmul(ps[:, 4 + n, 0:T], PERM, QP[:, n, :], start=True, stop=True)
        last.then_inc(sem("swap"), 1)
        pe.wait_ge(sem("kpe_out"), 1)
        nc.tensor.matmul(ps[:, 3, 0:T], PERM, KPE[:, :], start=True, stop=True).then_inc(sem("swap"), 1)
        c0 = PHASES["uk"]
        h = c0 % SPLIT_SLOTS
        pe.wait_ge(chunk_split, c0 + 1)
        pe.wait_ge(sem("ck_low"), 1)
        for n in range(HEADS):
            if n >= 3:
                pe.wait_ge(sem("k_out"), n - 2)
            for k in range(2):
                w = slice(k * 1024 + n * P, k * 1024 + n * P + P)
                last = product(ps[:, n % 3, 0:KEYS], WH[:, h, w], WL[:, h, w], CKH[:, k, 0:KEYS],
                               CKL[:, k, 0:KEYS], k == 0, k == 1)
            last.then_inc(sem("k_mm") if n < HEADS - 1 else chunk_used, 1)
        c1 = PHASES["uv"]
        h1 = c1 % SPLIT_SLOTS
        pe.wait_ge(chunk_split, c1 + 1)
        pe.wait_ge(sem("k_out"), HEADS)
        for n in range(8):
            t, half = n // 2, n % 2
            if n >= 3:
                pe.wait_ge(sem("v_out"), n - 2)
            for k in range(2):
                w = slice(k * 1024 + half * 512, k * 1024 + half * 512 + 512)
                kh, kl = CKH[:, k, t * P:(t + 1) * P], CKL[:, k, t * P:(t + 1) * P]
                nc.tensor.matmul(ps[:, n % 3, :], kh, WH[:, h1, w], start=k == 0, stop=False)
                nc.tensor.matmul(ps[:, n % 3, :], kh, WL[:, h1, w], start=False, stop=False)
                last = nc.tensor.matmul(ps[:, n % 3, :], kl, WH[:, h1, w], start=False, stop=k == 1)
            last.then_inc(sem("v_mm") if n < 7 else chunk_used, 1)
        pe.wait_ge(sem("v_out"), 8)
        pe.wait_ge(sem("roped"), 2)
        for t, (c, rows) in enumerate(((0, 128), (128, 128), (384, 32))):
            for k in range(2):
                nc.tensor.transpose(ps[0:rows, t, k * P:k * P + P], CKT[:, k, c:c + rows], ID)
            last = nc.tensor.transpose(ps[0:rows, t, 256:256 + ROPE], KP[0:ROPE, c:c + rows], ID[0:ROPE, 0:ROPE])
        last.then_inc(sem("cacheT"), 1)

        def mla_scores(n):
            kind, h = MLA_UNITS[n]
            bank = 4 + n % 3
            if n >= 3:
                pe.wait_ge(sem("mla_sm"), n - 2)
            if kind == "p":
                for t in range(2):
                    q = slice(t * P, (t + 1) * P)
                    po = 64 * (h % 2)
                    out = ps[:, bank, t * 256:(t + 1) * 256]
                    nc.tensor.matmul(out, QN[:, h, q], KN[:, h, 0:TP], start=True, stop=False)
                    last = nc.tensor.matmul(out, QP[po:po + 64, h // 2, q], KP[po:po + 64, 0:TP], start=False,
                                            stop=True)
            else:
                for j in range(4):
                    hh = 4 * h + j
                    po = 64 * (hh % 2)
                    out = ps[32 * j:32 * j + 32, bank, 0:PAST + TS]
                    nc.tensor.matmul(out, QN[:, hh, TP:T], KN[:, hh, TP:KEYS], start=True, stop=False)
                    last = nc.tensor.matmul(out, QP[po:po + 64, hh // 2, TP:T], KP[po:po + 64, TP:KEYS],
                                            start=False, stop=True)
            last.then_inc(sem("mla_s"), 1)

        def mla_turn(n):
            kind, h = MLA_UNITS[n]
            pe.wait_ge(sem("mla_p"), n + 1)
            if n >= 1:
                pe.wait_ge(sem("mla_pt"), n)
            sm = SM[n % 2]
            if kind == "p":
                for t in range(2):
                    for k in range(2):
                        last = nc.tensor.transpose(ps[:, 7, k * 256 + t * P:k * 256 + t * P + P],
                                                   sm[:, t * 256 + k * P:t * 256 + k * P + P], ID)
            else:
                nc.tensor.transpose(ps[:, 7, 0:P], sm[:, 0:P], ID)
                last = nc.tensor.transpose(ps[0:TS, 7, P:2 * P], sm[:, P:P + TS], ID)
            last.then_inc(sem("mla_t"), 1)

        def mla_sum(n):
            kind, h = MLA_UNITS[n]
            pt = PT[n % 2]
            pe.wait_ge(sem("mla_pt"), n + 1)
            if n >= 2:
                pe.wait_ge(sem("mla_ol"), n - 1)
            bank = n % 2
            if kind == "p":
                for k in range(2):
                    last = nc.tensor.matmul(ps[:, bank, 0:TP], VV[:, k, h * P:(h + 1) * P],
                                            pt[:, k * 256:(k + 1) * 256], start=k == 0, stop=k == 1)
            else:
                for j in range(4):
                    hh = 4 * h + j
                    out = ps[:, bank, 32 * j:32 * j + 32]
                    nc.tensor.matmul(out, VV[:, 2, hh * P:(hh + 1) * P], pt[:, 32 * j:32 * j + 32], start=True,
                                     stop=False)
                    last = nc.tensor.matmul(out, VV[0:TS, 3, hh * P:(hh + 1) * P],
                                            pt[0:TS, P + 32 * j:P + 32 * j + 32], start=False, stop=True)
            last.then_inc(sem("mla_o"), 1)

        pe.wait_ge(sem("cacheT_out"), 1)
        NU = len(MLA_UNITS)
        mla_scores(0)
        mla_scores(1)
        for n in range(NU):
            if n + 2 < NU:
                mla_scores(n + 2)
            mla_turn(n)
            if n >= 1:
                mla_sum(n - 1)
        mla_sum(NU - 1)

        pe.wait_ge(sem("rec_low"), 1)
        pe.wait_ge(sem("mla_ol"), NU)
        residual_linear("wout", lambda i, s: linear_body("wout", i, sums=s), 4)
        variance("ln00")

        def cross_attention(l):
            name = f"wq{l}"
            with pe.Fori(0, 4) as i:
                linear_body(name, i, ln=f"ln{l}0")
            x = f"xa{l}"

            def key_tiles(h):
                pe.wait_ge(*reached(f"{x}_kin{h % 2}", 32 * (h // 2 + 1)))
                for k in range(4):
                    n = 4 * h + k
                    if n >= 2:
                        pe.wait_ge(*reached(f"{x}_kt", n - 1))
                    for t in range(4):
                        last = nc.tensor.transpose(ps[:, n % 2, t * P:(t + 1) * P],
                                                   KNAT[h % 2][:, t, k * P:(k + 1) * P], ID)
                    last.then_inc(sem(f"{x}_ktT"), 1)

            def scores(h):
                pe.wait_ge(*reached(f"{x}_kt", 4 * h + 4))
                if h >= 2:
                    pe.wait_ge(*reached(f"{x}_sm", h - 1))
                kt = KT[h % 2]
                for t in range(2):
                    for k in range(4):
                        nc.tensor.matmul(ps[:, 4 + h % 2, t * 256:(t + 1) * 256], QX[:, 4 * h + k, t * P:(t + 1) * P],
                                         kt[:, k, 0:256], start=k == 0, stop=k == 3)
                for k in range(4):
                    last = nc.tensor.matmul(ps[32 * h:32 * h + 32, 6, 0:256], QX[:, 4 * h + k, TP:T],
                                            kt[:, k, 256:512], start=k == 0, stop=k == 3)
                last.then_inc(sem(f"{x}_s"), 1)

            def turn(n):
                pe.wait_ge(*reached(f"{x}_p", n + 1))
                if n >= 1:
                    pe.wait_ge(*reached(f"{x}_pt", n))
                for t in range(2 if n < 4 else 1):
                    for k in range(2):
                        last = nc.tensor.transpose(ps[:, 7, k * 256 + t * P:k * 256 + t * P + P],
                                                   SX[n % 2][:, t * 256 + k * P:t * 256 + k * P + P], ID)
                last.then_inc(sem(f"{x}_t"), 1)

            def weighted(n):
                pe.wait_ge(*reached(f"{x}_pt", n + 1))
                if n >= 1:
                    pe.wait_ge(*reached(f"{x}_ol", n))
                pt = PX[n % 2]
                if n < 4:
                    pe.wait_ge(*reached(f"{x}_vin{n % 2}", 16 * (n // 2 + 1)))
                    for m in range(4):
                        for k in range(2):
                            last = nc.tensor.matmul(ps[:, 2 + m // 2, (m % 2) * 256:(m % 2) * 256 + 256],
                                                    VP[n % 2][:, k, m * P:(m + 1) * P], pt[:, k * 256:(k + 1) * 256],
                                                    start=k == 0, stop=k == 1)
                else:
                    pe.wait_ge(*reached(f"{x}_vs", 16))
                    for m in range(NK):
                        for k in range(2):
                            last = nc.tensor.matmul(ps[:, 2, m * 32:(m + 1) * 32], VS[:, k, m * P:(m + 1) * P],
                                                    pt[:, k * 256 + 32 * (m // 4):k * 256 + 32 * (m // 4) + 32],
                                                    start=k == 0, stop=k == 1)
                last.then_inc(sem(f"{x}_o"), 1)

            for b in range(2):
                pe.wait_ge(*reached(f"wq{l}_out{b}", 4))
            key_tiles(0)
            scores(0)
            for h in range(4):
                if h < 3:
                    key_tiles(h + 1)
                    scores(h + 1)
                turn(h)
                weighted(h)
            turn(4)
            weighted(4)
            pe.wait_ge(*reached(f"{x}_ol", 5))
            residual_linear(f"wo{l}", lambda i, s: linear_body(f"wo{l}", i, sums=s), 4)
            variance(f"ln{l}1")

        def mlp(l):
            for half, (up, dn) in enumerate((("upa", "downa"), ("upb", "downb"))):
                with pe.Fori(0, 8) as i:
                    linear_body(f"{up}{l}", i, ln=f"ln{l}1")
                for b in range(2):
                    pe.wait_ge(*reached(f"{up}{l}_low{b}", 8))
                if half == 0:
                    with pe.Fori(0, 4) as i:
                        down_body(f"{dn}{l}", i)
                    for b in range(2):
                        pe.wait_ge(*reached(f"{dn}{l}_out{b}", 4))
                else:
                    residual_linear(f"{dn}{l}", lambda i, s: down_body(f"{dn}{l}", i, s), 4)
            variance(f"ln{l}2")

        cross_attention(0)
        mlp(0)

        pe.wait_ge(sem("pool_in"), 16)
        for k in range(NK):
            last = nc.tensor.transpose(ps[:, 6, k * PBUF:(k + 1) * PBUF], SPN[0:PBUF, k * P:(k + 1) * P],
                                       ID[0:PBUF, 0:PBUF])
        last.then_inc(sem("poolT"), 1)
        c0 = PHASES["pool"]
        for g in range(4):
            pe.wait_ge(sem("pool_low"), g + 1)
            pe.wait_ge(chunk_split, c0 + g + 1)
            if g >= 1:
                pe.wait_ge(sem("pool_x"), 4 * g)
                static_sums("pool", range(4 * g - 4, 4 * g), g == 1, False)
            for k in range(4):
                for m in range(4):
                    w = slice(k * 512 + m * P, k * 512 + m * P + P)
                    last = product(ps[:, m, 0:T], WH[:, (c0 + g) % 2, w], WL[:, (c0 + g) % 2, w],
                                   XH[:, 4 * g + k, :], XL[:, 4 * g + k, :], k == 0, k == 3)
            last.then_inc(chunk_used, 1)
        pe.wait_ge(sem("poolT_out"), 1)
        for n in range(8):
            if n >= 2:
                pe.wait_ge(sem("pst_out"), n - 1)
            for k in range(4):
                kk = 4 * (n % 4) + k
                c = PBUF + TP - PBUF if n < 4 else EW - PBUF
                last = nc.tensor.transpose(ps[0:PBUF, 6 + n % 2, k * P:(k + 1) * P], EXT[:, kk, c:c + PBUF], ID)
            last.then_inc(sem("pstT"), 1)
        pe.wait_ge(sem("pool_x"), 16)
        static_sums("pool", range(12, 16), False, True).then_inc(sem("pool_sum"), 1)
        pe.wait_ge(sem("pst_out"), 8)
        variance("ln10")
        cross_attention(1)
        mlp(1)
        for n in range(12):
            t, q = n // 4, n % 4
            rows = 128 if t < 2 else 32
            pe.wait_ge(*reached("ln12_x", 4 * q + 4))
            if n >= 4:
                pe.wait_ge(sem("y_out"), n - 3)
            for k in range(4):
                last = nc.tensor.transpose(ps[0:rows, n % 4, k * P:(k + 1) * P],
                                           X[:, 4 * q + k, t * P:t * P + rows], ID)
            last.then_inc(sem("yT"), 1)

    @block.scalar
    def _(act):
        A = nc.scalar.activation
        act.dma_start(CST[:, :], a["cst"]).then_inc(sem("cst_in"), 16)
        act.dma_start(MIN[:, 0, :], a["mem_prompt"][0][0:P, :]).then_inc(sem("mem_in"), 16)
        act.dma_start(MIN[:, 1, :], a["mem_prompt"][0][P:2 * P, :]).then_inc(sem("mem_in"), 16)
        rows = lambda t, r0, n: PN[r0:r0 + n, t, :]
        for dst, src in (
                (rows(0, 0, 96), a["ln_g"].rearrange("l s (k c) -> (l s k) c", c=P)),
                (rows(1, 0, 96), a["ln_b"].rearrange("l s (k c) -> (l s k) c", c=P)),
                (rows(2, P_CONVW, 32), a["conv_w"][0].rearrange("w (k c) -> (w k) c", c=P)),
                (rows(2, P_CONVB, 8), a["conv_b"][0].rearrange("(k c) -> k c", c=P)),
                (rows(2, P_GAB, 8), a["gate_a_b"][0]),
                (rows(2, P_GXB, 8), a["gate_x_b"][0]),
                (rows(2, P_LAM, 8), a["lru_lambda"][0].rearrange("(k c) -> k c", c=P)),
                (rows(2, P_H0, 8), a["state_rglru_h"][0, 0].rearrange("(k c) -> k c", c=P)),
                (rows(2, P_CST, 24), a["state_rglru_conv"][0, 0].rearrange("w (k c) -> (w k) c", c=P)),
                (rows(2, P_PSC, 16), a["pool_scale"][0].rearrange("(k c) -> k c", c=P)),
                (rows(2, P_QN, 4), a["q_norm_g"][0].rearrange("(k c) -> k c", c=P)),
                (rows(2, P_KN, 2), a["kv_norm_g"][0].rearrange("(k c) -> k c", c=P))):
            act.dma_start(dst, src).then_inc(sem("par_in"), 16)
        act.dma_start(XIN[:, 0, :], a["x_prompt"][0][0:P, :]).then_inc(sem("x_in"), 16)
        act.dma_start(XIN[:, 1, :], a["x_prompt"][0][P:2 * P, :]).then_inc(sem("x_in"), 16)
        act.dma_start(XIN[0:TS, 2, :], a["x_sample"][0]).then_inc(sem("x_in"), 16)
        for r in range(8):
            act.wait_ge(sem("memT"), r + 1)
            A(MTH[:, 2 * r:2 * r + 2, :].rearrange("p k n -> p (k n)"), ps[:, 4 + r % 4, :], ACT.Copy
              ).then_inc(sem("memT_high"), 1)
        act.wait_ge(sem("parT"), 1)
        for t, (n, c) in enumerate(((96, 0), (96, 96), (118, 192))):
            last = A(PR[:, c:c + n], ps[:, 4, t * P:t * P + n], ACT.Copy)
        last.then_inc(sem("par_done"), 1)
        for k in range(NK):
            act.wait_ge(sem("xT"), k + 1)
            A(XH[:, k, :], ps[:, 4 + k % 4, 0:T], ACT.Copy).then_inc(sem("xT_high"), 1)
            A(X[:, k, :], ps[:, 4 + k % 4, 0:T], ACT.Copy).then_inc(sem("xT_x"), 1)
        for l in range(2):
            with act.Fori(0, 4) as i:
                for half in range(2):
                    act.wait_ge(chunk_used, PHASES[f"mem{l}"] + 4 * half + 4 + 8 * i)
                    act.wait_ge(sem(f"mem_stored{half}"), 16 * i + 64 * l)
                    A(STG[:, half, :], ps[:, 2 * half:2 * half + 2, :].rearrange("p t n -> p (t n)"), ACT.Copy
                      ).then_inc(sem(f"mem_out{half}"), 1)
                    act.wait_ge(sem(f"mem_out{half}"), i + 4 * l + 1)
                    dst = o["p_mem_k" if half == 0 else "p_mem_v"][l, 0].rearrange("(t p) n -> p t n", p=P)
                    act.dma_start(dst[:, :, ds(i * 512, 512)], STG[:, half, :].rearrange("p (t n) -> p t n", t=2)
                                  ).then_inc(sem(f"mem_stored{half}"), 16)

        act.wait_ge(sem("pads"), 2)
        with act.Fori(0, 2) as i:
            for b in range(2):
                act.wait_ge(chunk_used, PHASES["u"] + 2 * b + 2 + 4 * i)
                A(UE[:, ds(i * 4 + 2 * b, 2), 3:3 + TP], ps[:, 2 * b:2 * b + 2, 0:TP], ACT.Copy)
                A(UE[:, ds(i * 4 + 2 * b, 2), 6 + TP:UW], ps[:, 2 * b:2 * b + 2, TP:T], ACT.Copy
                  ).then_inc(sem(f"u_out{b}"), 1)
        for half in range(2):
            act.wait_ge(sem(f"mem_stored{half}"), 16 * 8)
        with act.Fori(0, 2) as i:
            for b in range(2):
                act.wait_ge(chunk_used, PHASES["gate"] + 2 * b + 2 + 4 * i)
                A(GT[:, ds(i * 4 + 2 * b, 2), :], ps[:, 2 * b:2 * b + 2, 0:T], ACT.Gelu_apprx_tanh
                  ).then_inc(sem(f"gate_out{b}"), 1)
        act.wait_ge(sem("sp_abs"), 1)
        A(SMALL[:, 72:80], SMALL[:, 64:72], ACT.Exp, scale=-1.0).then_inc(sem("sp_exp"), 1)
        for n in range(2 * LT):
            act.wait_ge(sem("gate_mm"), n + 1)
            m = n % LT
            A((RR if n < LT else IG)[:, m, 0:CW], ps[:, 4 + n % 4, 0:CW], ACT.Sigmoid,
              bias=col((P_GAB if n < LT else P_GXB) + m)).then_inc(sem("gates_sig"), 1)
        act.wait_ge(sem("gates_sig"), 2 * LT)
        act.wait_ge(sem("sp_done"), 1)
        act.wait_ge(sem("state_cols"), 2)
        for m in range(LT):
            A(TT[:, m, :], RR[:, m, 0:CW], ACT.Tanh, scale=SMALL[:, 88 + m:89 + m]).then_inc(sem("tanh"), 1)
        act.wait_ge(sem("tanh"), LT)
        for m in range(LT):
            A(RR[:, m, 0:CW], RR[:, m, 0:CW], ACT.Exp, scale=SMALL[:, 96 + m:97 + m]).then_inc(sem("decay"), 1)
        act.wait_ge(chunk_used, PHASES["cq"] + 2)
        A(CQ[:, 0:2, :], ps[:, 0:2, 0:T], ACT.Copy).then_inc(sem("cq_out0"), 1)
        act.wait_ge(chunk_used, PHASES["cq"] + 4)
        A(CQ[:, 2:4, :], ps[:, 2:4, 0:T], ACT.Copy).then_inc(sem("cq_out1"), 1)
        act.wait_ge(sem("cq_out0"), 1)
        act.wait_ge(sem("cq_out1"), 1)
        A(SQM[:, :, :], CQ[:, :, :], ACT.Square).then_inc(sem("sq_q"), 1)
        act.wait_ge(chunk_used, PHASES["ckv"] + 2)
        A(CKV[:, :, :], ps[:, 0:2, 0:T], ACT.Copy).then_inc(sem("ckv_out"), 1)
        act.wait_ge(chunk_used, PHASES["kpe"] + 1)
        A(KPE[:, :], ps[:, 2, 0:T], ACT.Copy).then_inc(sem("kpe_out"), 1)
        act.wait_ge(sem("rec_ratio"), 1)
        A(TT[:, :, :], TT[:, :, :], ACT.Sqrt).then_inc(sem("rec_root"), 1)
        act.wait_ge(sem("ckv_out"), 1)
        act.wait_ge(sem("ssum"), 1)
        A(SQM[:, 0:2, :], CKV[:, :, :], ACT.Square).then_inc(sem("sq_kv"), 1)
        for n in range(2):
            act.wait_ge(sem("rms_eps"), n + 1)
            r = RS[:, :] if n == 0 else RELU[:, 0, :]
            A(r, r, ACT.Sqrt).then_inc(sem("rms_root"), 1)
        act.wait_ge(sem("rec"), 1)
        act.wait_ge(chunk_used, PHASES["kpe"] + 1)
        A(XH[:, 0:LT, :], GT[:, :, :], ACT.Copy).then_inc(sem("rec_high"), 1)
        act.wait_ge(sem("stateT"), 1)
        A(SMALL[0:64, 128:256], ps[0:64, 7, 0:P], ACT.Copy).then_inc(sem("stateT_out"), 1)
        act.wait_ge(sem("stateT_out"), 1)
        for r, n, dst in ((0, 24, o["p_conv"][0, 0].rearrange("w (k c) -> (w k) c", c=P)),
                          (24, 24, o["s_conv"][0, 0].rearrange("w (k c) -> (w k) c", c=P)),
                          (48, 8, o["p_h"][0, 0].rearrange("(k c) -> k c", c=P)),
                          (56, 8, o["s_h"][0, 0].rearrange("(k c) -> k c", c=P))):
            act.dma_start(dst, SMALL[r:r + n, 128:256]).then_inc(sem("stored"), 16)
        act.wait_ge(sem("cq_n"), 4)
        act.wait_ge(sem("rec_low"), 1)
        A(CQH[:, :, :], CQ[:, :, :], ACT.Copy).then_inc(sem("cq_high"), 1)
        act.wait_ge(sem("pastT"), 1)
        act.wait_ge(sem("ck_zero"), 1)
        A(CKT[:, :, TP:TP + PAST], ps[:, 6, 0:2 * P].rearrange("p (k n) -> p k n", k=2), ACT.Copy
          ).then_inc(sem("pastT_out"), 1)
        A(KP[:, TP:TP + PAST], ps[:, 6, 2 * P:3 * P], ACT.Copy).then_inc(sem("pastT_out"), 1)
        act.wait_ge(sem("pastT_out"), 2)
        act.wait_ge(sem("ck_n"), 4)
        A(CKH[:, :, :], CKT[:, :, :], ACT.Copy).then_inc(sem("ck_high"), 1)
        for n in range(4):
            act.wait_ge(chunk_used, PHASES["uq"] + n + 1)
            A(QN[:, 2 * n:2 * n + 2, :], ps[:, 0:2, 0:T], ACT.Copy)
            A(QP[:, n, :], ps[:, 2, 0:T], ACT.Copy).then_inc(sem("q_out"), 1)
        for n in range(HEADS):
            if n < HEADS - 1:
                act.wait_ge(sem("k_mm"), n + 1)
            else:
                act.wait_ge(chunk_used, PHASES["uk"] + 1)
            A(KN[:, n, :], ps[:, n % 3, 0:KEYS], ACT.Copy).then_inc(sem("k_out"), 1)
        act.wait_ge(sem("cq_low"), 1)
        for n in range(8):
            if n < 7:
                act.wait_ge(sem("v_mm"), n + 1)
            else:
                act.wait_ge(chunk_used, PHASES["uv"] + 1)
            A(VV[:, n // 2, (n % 2) * 512:(n % 2) * 512 + 512], ps[:, n % 3, :], ACT.Copy).then_inc(sem("v_out"), 1)
        act.wait_ge(sem("cacheT"), 1)
        for t in range(3):
            rows_ = 128 if t < 2 else 32
            last = A(OST[0:rows_, t, :], ps[0:rows_, t, 0:320], ACT.Copy)
        last.then_inc(sem("cacheT_out"), 1)
        act.wait_ge(sem("cacheT_out"), 1)
        act.dma_start(o["p_ckv"][0, 0].rearrange("(t p) n -> p t n", p=P), OST[:, 0:2, 0:256]).then_inc(sem("stored"), 16)
        act.dma_start(o["p_kpe"][0, 0].rearrange("(t p) n -> p t n", p=P), OST[:, 0:2, 256:320]).then_inc(sem("stored"), 16)
        act.dma_start(o["s_ckv"][0, 0], OST[0:TS, 2, 0:256]).then_inc(sem("stored"), 16)
        act.dma_start(o["s_kpe"][0, 0], OST[0:TS, 2, 256:320]).then_inc(sem("stored"), 16)

        def softmax(kind, n, x, sm, scale, width):
            act.wait_ge(*reached(f"{x}_max", n + 1))
            sl = 256 + 8 * (n % 2)
            for t in range(2 if kind == "p" else 1):
                last = A(sm[:, t * 256:t * 256 + width], sm[:, t * 256:t * 256 + width], ACT.Exp, scale=scale,
                         bias=SMALL[:, sl + 2 + t:sl + 3 + t], accum_out=SMALL[:, sl + 4 + t:sl + 5 + t])
            last.then_inc(sem(f"{x}_exp"), 1)

        def mla_out(n):
            kind, h = MLA_UNITS[n]
            act.wait_ge(sem("mla_t"), n + 1)
            if n >= 2:
                act.wait_ge(sem("mla_o"), n - 1)
            if kind == "p":
                A(PT[n % 2][:, :], ps[:, 7, :], ACT.Copy).then_inc(sem("mla_pt"), 1)
            else:
                A(PT[n % 2][:, 0:P], ps[:, 7, 0:P], ACT.Copy)
                A(PT[n % 2][0:TS, P:2 * P], ps[0:TS, 7, P:2 * P], ACT.Copy).then_inc(sem("mla_pt"), 1)

        def mla_high(n):
            kind, h = MLA_UNITS[n]
            act.wait_ge(sem("mla_o"), n + 1)
            if kind == "p":
                A(XH[:, LT + h, 0:TP], ps[:, n % 2, 0:TP], ACT.Copy).then_inc(sem("mla_oh"), 1)
            else:
                A(XH[:, LT + 4 * h:LT + 4 * h + 4, TP:T], ps[:, n % 2, 0:P].rearrange("p (h n) -> p h n", h=4),
                  ACT.Copy).then_inc(sem("mla_oh"), 1)

        NU = len(MLA_UNITS)
        for n in range(NU):
            softmax(MLA_UNITS[n][0], n, "mla", SM[n % 2], MLA_SCALE, 256 if MLA_UNITS[n][0] == "p" else PAST + TS)
            mla_out(n)
            if n >= 1:
                mla_high(n - 1)
        mla_high(NU - 1)

        def ln(name, l, s, high=True):
            for q in range(4):
                act.wait_ge(*reached(f"{name}_d", q + 1))
                A(SQ[:, 4 * q:4 * q + 4, :], X[:, 4 * q:4 * q + 4, :], ACT.Square).then_inc(sem(f"{name}_sq"), 1)
            act.wait_ge(*reached(f"{name}_eps", 1))
            A(RS[:, :], RS[:, :], ACT.Sqrt).then_inc(sem(f"{name}_root"), 1)
            if high:
                for k in range(NK):
                    act.wait_ge(*reached(f"{name}_t", k + 1))
                    A(XH[:, k, :], X[:, k, :], ACT.Identity, bias=LNB(l, s, k)).then_inc(sem(f"{name}_high"), 1)
                for k in range(NK):
                    act.wait_ge(*reached(f"{name}_low", k // 4 + 1))
                    A(X[:, k, :], X[:, k, :], ACT.Identity, bias=LNB(l, s, k)).then_inc(sem(f"{name}_x"), 1)
            else:
                for k in range(NK):
                    act.wait_ge(*reached(f"{name}_t", k + 1))
                    A(X[:, k, :], X[:, k, :], ACT.Identity, bias=LNB(l, s, k)).then_inc(sem(f"{name}_x"), 1)

        def cross_attention(l):
            x = f"xa{l}"
            with act.Fori(0, 4) as i:
                for b in range(2):
                    act.wait_ge(chunk_used, PHASES[f"wq{l}"] + 2 * b + 2 + 4 * i)
                    A(QX[:, ds(i * 4 + 2 * b, 2), :], ps[:, 2 * b:2 * b + 2, 0:T], ACT.Copy
                      ).then_inc(sem(f"wq{l}_out{b}"), 1)

            def keys(h):
                for k in range(4):
                    act.wait_ge(*reached(f"{x}_ktT", 4 * h + k + 1))
                    if h >= 2 and k == 0:
                        act.wait_ge(*reached(f"{x}_s", h - 1))
                    A(KT[h % 2][:, k, :], ps[:, k % 2, :], ACT.Copy).then_inc(sem(f"{x}_kt"), 1)

            def out(n):
                act.wait_ge(*reached(f"{x}_t", n + 1))
                if n >= 2:
                    act.wait_ge(*reached(f"{x}_o", n - 1))
                if n < 4:
                    A(PX[n % 2][:, :], ps[:, 7, :], ACT.Copy).then_inc(sem(f"{x}_pt"), 1)
                else:
                    A(PX[0].rearrange("p (k n) -> p k n", k=2)[:, :, 0:P],
                      ps[:, 7, :].rearrange("p (k n) -> p k n", k=2)[:, :, 0:P], ACT.Copy).then_inc(sem(f"{x}_pt"), 1)

            def high(n):
                act.wait_ge(*reached(f"{x}_o", n + 1))
                if n < 4:
                    A(XH[:, 4 * n:4 * n + 4, 0:TP], ps[:, 2:4, :].rearrange("p b (m n) -> p (b m) n", m=2),
                      ACT.Copy).then_inc(sem(f"{x}_oh"), 1)
                else:
                    A(XH[:, :, TP:T], ps[:, 2, :].rearrange("p (m n) -> p m n", m=NK), ACT.Copy
                      ).then_inc(sem(f"{x}_oh"), 1)

            keys(0)
            for h in range(4):
                if h < 3:
                    keys(h + 1)
                softmax("p", h, x, SX[h % 2], XA_SCALE, 256)
                out(h)
                high(h)
            softmax("s", 4, x, SX[0], XA_SCALE, 256)
            out(4)
            high(4)

        def mlp(l):
            for up in ("upa", "upb"):
                with act.Fori(0, 8) as i:
                    for b in range(2):
                        name = f"{up}{l}"
                        act.wait_ge(chunk_used, PHASES[name] + 2 * b + 2 + 4 * i)
                        A(RELU[:, :, :], ps[:, 2 * b:2 * b + 2, 0:T], ACT.Relu).then_inc(sem(f"{name}_out{b}"), 1)
                        act.wait_ge(*reached(f"{name}_out{b}", i + 1))
                        act.wait_ge(*reached(f"{name}_low{b}", i))
                        A(SQH[:, b, :, :], RELU[:, :, :], ACT.Square)
                        A(HH[:, ds(i * 4 + 2 * b, 2), :], RELU[:, :, :], ACT.Square).then_inc(sem(f"{name}_high{b}"), 1)
            ln(f"ln{l}2", l, 2, high=False)

        ln("ln00", 0, 0)
        cross_attention(0)
        ln("ln01", 0, 1)
        mlp(0)
        act.wait_ge(sem("ext_zero"), 1)
        act.wait_ge(*reached("ln02_x", NK))
        for q in range(4):
            A(EXT[:, 4 * q:4 * q + 4, PBUF:PBUF + TP], X[:, 4 * q:4 * q + 4, 0:TP], ACT.Copy)
            A(EXT[:, 4 * q:4 * q + 4, 2 * PBUF + TP:EW], X[:, 4 * q:4 * q + 4, TP:T], ACT.Copy).then_inc(sem("ext"), 1)
        act.wait_ge(sem("poolT"), 1)
        A(EXT[:, :, PBUF + TP:2 * PBUF + TP], ps[:, 6, 0:NK * PBUF].rearrange("p (k n) -> p k n", k=NK), ACT.Copy
          ).then_inc(sem("poolT_out"), 1)
        for g in range(4):
            act.wait_ge(sem("pool_d"), g + 1)
            A(XH[:, 4 * g:4 * g + 4, :], SQH[:, :, :, :].rearrange("p a b n -> p (a b) n"), ACT.Copy).then_inc(sem("pool_high"), 1)
        for g in range(4):
            act.wait_ge(chunk_used, PHASES["pool"] + g + 1)
            for m in range(4):
                n = 4 * g + m
                if n >= 2:
                    act.wait_ge(sem("pool_x"), n - 1)
                A(RELU[:, n % 2, :], ps[:, m, 0:T], ACT.Copy, scale=col(P_PSC + n)).then_inc(sem("pool_y"), 1)
        for n in range(8):
            act.wait_ge(sem("pstT"), n + 1)
            act.wait_ge(sem("pool_low"), 4)
            A(PST[0:PBUF, n // 4, (n % 4) * 512:(n % 4) * 512 + 512], ps[0:PBUF, 6 + n % 2, :], ACT.Copy
              ).then_inc(sem("pst_out"), 1)
        act.wait_ge(sem("pst_out"), 8)
        act.dma_start(o["p_pool"][0, 0], PST[0:PBUF, 0, :]).then_inc(sem("stored"), 16)
        act.dma_start(o["s_pool"][0, 0], PST[0:PBUF, 1, :]).then_inc(sem("stored"), 16)
        ln("ln10", 1, 0)
        cross_attention(1)
        ln("ln11", 1, 1)
        mlp(1)
        for n in range(12):
            t, q = n // 4, n % 4
            rows_ = 128 if t < 2 else 32
            act.wait_ge(sem("yT"), n + 1)
            A(YST[0:rows_, t, q * 512:(q + 1) * 512], ps[0:rows_, n % 4, :], ACT.Copy).then_inc(sem("y_out"), 1)
            if q == 3:
                act.wait_ge(sem("y_out"), n + 1)
                dst = o["y_prompt"][0][t * P:(t + 1) * P, :] if t < 2 else o["y_sample"][0]
                act.dma_start(dst, YST[0:rows_, t, :]).then_inc(sem("stored"), 16)
        act.wait_ge(sem("stored"), 16 * 13)
        for half in range(2):
            act.wait_ge(sem(f"mem_stored{half}"), 16 * 8)

    @block.gpsimd
    def _(pool):
        G = nc.gpsimd
        G.memset(ONES[:, :], 1.0 / D).then_inc(sem("ones"), 1)
        pool.wait_ge(sem("xT"), NK)
        pool.wait_ge(sem("par_done"), 1)
        G.memset(UE[:, :, 0:3], 0.0).then_inc(sem("pads"), 1)
        G.tensor_copy(UE[:, :, 3 + TP:6 + TP],
                      PR[:, R0 + P_CST:R0 + P_CST + 24].rearrange("p (w k) -> p k w", k=LT)).then_inc(sem("pads"), 1)
        pool.wait_ge(chunk_used, PHASES["mem1"] + 32)
        G.dma_start(GW[:, 0:LT, :], a["gate_a_w"][0].rearrange("h i j -> i h j")).then_inc(sem("gates_in"), 16)
        G.dma_start(GW[:, LT:2 * LT, :], a["gate_x_w"][0].rearrange("h i j -> i h j")).then_inc(sem("gates_in"), 16)
        G.dma_start(CPN[:, 0:KVL], a["cache_mla_ckv"][0, 0]).then_inc(sem("past_in"), 16)
        for h in range(2):
            G.dma_start(CPN[:, KVL + h * ROPE:KVL + (h + 1) * ROPE], a["cache_mla_kpe"][0, 0]
                        ).then_inc(sem("past_in"), 16)
        for half in range(2):
            pool.wait_ge(sem(f"mem_stored{half}"), 16 * 8)
        for b in range(2):
            pool.wait_ge(sem(f"u_out{b}"), 2)
        for c, at in ((0, TP), (24, UW - 3)):
            G.tensor_copy(SMALL[:, c:c + 24].rearrange("p (w k) -> p k w", k=LT), UE[:, :, at:at + 3]
                          ).then_inc(sem("state_cols"), 1)
        pool.wait_ge(sem("gates_sig"), 2 * LT)
        G.tensor_tensor(IG[:, :, 0:CW], IG[:, :, 0:CW], UC[:, :, 0:CW], ALU.mult).then_inc(sem("gated"), 1)

        def memory(l):
            x = f"xa{l}"
            kd = (o["p_mem_k"][l, 0], a["cache_mem_k"][l, 0])
            vd = (o["p_mem_v"][l, 0], a["cache_mem_v"][l, 0])

            def keys(h):
                if h >= 2:
                    pool.wait_ge(*reached(f"{x}_ktT", 4 * (h - 1)))
                for n in range(2):
                    G.dma_start(KNAT[h % 2][:, 2 * n:2 * n + 2, :],
                                kd[n].rearrange("(t p) n -> p t n", p=P)[:, :, h * 512:(h + 1) * 512]
                                ).then_inc(sem(f"{x}_kin{h % 2}"), 16)

            def values(h):
                if h >= 2:
                    pool.wait_ge(*reached(f"{x}_o", h - 1))
                G.dma_start(VP[h % 2][:, :, :], vd[0].rearrange("(t p) n -> p t n", p=P)[:, :, h * 512:(h + 1) * 512]
                            ).then_inc(sem(f"{x}_vin{h % 2}"), 16)

            keys(0)
            keys(1)
            values(0)
            values(1)
            keys(2)
            keys(3)
            values(2)
            pool.wait_ge(*reached(f"{x}_ktT", 16))
            G.dma_start(VS[:, :, :], vd[1].rearrange("(t p) n -> p t n", p=P)).then_inc(sem(f"{x}_vs"), 16)
            values(3)

        pool.wait_ge(sem("mla_o"), len(MLA_UNITS))
        memory(0)
        pool.wait_ge(chunk_used, PHASES["downb0"] + 32)
        G.dma_start(SPN[0:PBUF, :], a["state_pool"][0, 0]).then_inc(sem("pool_in"), 16)
        pool.wait_ge(*reached("ln02_var", 1))
        G.memset(EXT[:, :, 0:PBUF], 0.0).then_inc(sem("ext_zero"), 1)
        pool.wait_ge(sem("stored"), 16 * 10)
        pool.wait_ge(sem("pool_low"), 4)
        memory(1)

    @block.vector
    def _(dve):
        V = nc.vector
        chained = [0]

        def chain(ins):
            chained[0] += 1
            ins.then_inc(sem("dve_step"), 1)
            dve.wait_ge(sem("dve_step"), chained[0])

        def split(c0, j, step=0, i=0):
            s, h = (c0 + j) % RAW_SLOTS, (c0 + j) % SPLIT_SLOTS
            dve.wait_ge(load_sem[s], loaded_count(c0 + j) + step * 4 * i)
            if c0 + j >= SPLIT_SLOTS or step:
                dve.wait_ge(chunk_used, c0 + j - SPLIT_SLOTS + 1 + step * i)
            V.tensor_copy(WH[:, h, :], RAW[:, s, :]).then_inc(split_hi, 1)
            dve.wait_ge(split_hi, c0 + j + 1 + step * i)
            V.tensor_tensor(WL[:, h, :], RAW[:, s, :], WH[:, h, :].bitcast(f32), ALU.subtract
                            ).then_inc(chunk_split, 1)

        def sub(out, x, high):
            return V.tensor_tensor(out, x, high.bitcast(f32), ALU.subtract)

        split(0, 0)
        for r in range(8):
            dve.wait_ge(sem("memT_high"), r + 1)
            sub(MTL[:, 2 * r:2 * r + 2, :].rearrange("p k n -> p (k n)"), ps[:, 4 + r % 4, :],
                MTH[:, 2 * r:2 * r + 2, :].rearrange("p k n -> p (k n)")).then_inc(sem("memT_low"), 1)
        split(0, 1)
        for k in range(NK):
            dve.wait_ge(sem("xT_x"), k + 1)
            sub(XL[:, k, :], ps[:, 4 + k % 4, 0:T], XH[:, k, :]).then_inc(sem("xT_low"), 1)
        for j in range(2, 9):
            split(0, j)
        with dve.Fori(1, 4) as i:
            for j in range(8):
                split(0, j + 1, 8, i)
        with dve.Fori(0, 4) as i:
            for j in range(8):
                split(PHASES["mem1"], j + 1, 8, i)
        with dve.Fori(0, 2) as i:
            for j in range(4):
                split(PHASES["u"], j + 1, 4, i)
        for j in range(8):
            split(PHASES["gate"], j + 1)
            k = j // 2
            if j == 0:
                dve.wait_ge(sem("pads"), 2)
                for b in range(2):
                    dve.wait_ge(sem(f"u_out{b}"), 2)
            for m in range(4 * (j % 2), 4 * (j % 2) + 4):
                w = col(P_CONVW + k * LT + m)
                if k == 0:
                    ins = V.tensor_scalar(UC[:, m, 0:CW], UE[:, m, 0:CW], w, col(P_CONVB + m), ALU.mult, ALU.add)
                else:
                    dve.wait_ge(sem("conv"), LT * (k - 1) + m + 1)
                    ins = V.scalar_tensor_tensor(out=UC[:, m, 0:CW], in0=UE[:, m, k:k + CW], scalar=w,
                                                 in1=UC[:, m, 0:CW], op0=ALU.mult, op1=ALU.add)
                ins.then_inc(sem("conv"), 1)
        lam = PR[:, R0 + P_LAM:R0 + P_LAM + LT]
        z = lambda n: SMALL[:, 64 + 8 * n:72 + 8 * n]
        V.scalar_tensor_tensor(out=z(0), in0=lam, scalar=-1.0, in1=lam, op0=ALU.mult, op1=ALU.max).then_inc(sem("sp_abs"), 1)
        dve.wait_ge(sem("sp_exp"), 1)
        chain(V.tensor_scalar(z(2), z(1), 2.0, None, ALU.add))
        chain(V.reciprocal(z(2), z(2)))
        chain(V.tensor_tensor(z(2), z(1), z(2), ALU.mult))
        chain(V.tensor_tensor(z(5), z(2), z(2), ALU.mult))
        chain(V.tensor_scalar(z(6), z(5), 1.0 / 17, None, ALU.mult))
        for d in (15, 13, 11, 9, 7, 5, 3):
            chain(V.scalar_tensor_tensor(out=z(6), in0=z(6), scalar=1.0 / d, in1=z(5), op0=ALU.add, op1=ALU.mult))
        chain(V.scalar_tensor_tensor(out=z(6), in0=z(6), scalar=1.0, in1=z(2), op0=ALU.add, op1=ALU.mult))
        chain(V.tensor_scalar(z(5), lam, -1.0, 0.0, ALU.mult, ALU.max))
        chain(V.scalar_tensor_tensor(out=z(6), in0=z(6), scalar=2.0, in1=z(5), op0=ALU.mult, op1=ALU.add))
        V.tensor_scalar(z(3), z(6), 8.0, None, ALU.mult)
        V.tensor_scalar(z(4), z(6), -8.0, None, ALU.mult).then_inc(sem("sp_done"), 1)
        for j in range(3):
            split(PHASES["cq"], j + 1)
        dve.wait_ge(sem("tanh"), LT)
        dve.wait_ge(sem("gated"), 1)
        chain(V.tensor_scalar(UC[:, :, 0:CW], TT[:, :, :], 1.0, None, ALU.add))
        chain(V.reciprocal(UC[:, :, 0:CW], UC[:, :, 0:CW]))
        split(PHASES["cq"], 4)
        V.scalar_tensor_tensor(out=TT[:, :, :], in0=TT[:, :, :], scalar=2.0, in1=UC[:, :, 0:CW], op0=ALU.mult,
                               op1=ALU.mult).then_inc(sem("rec_ratio"), 1)
        split(PHASES["ckv"], 1)
        split(PHASES["ckv"], 2)
        dve.wait_ge(sem("rec_root"), 1)
        dve.wait_ge(sem("decay"), LT)
        chain(V.tensor_tensor(IG[:, :, 0:CW], IG[:, :, 0:CW], TT[:, :, :], ALU.mult))
        for m in range(LT):
            V.tensor_tensor_scan(UC[:, m, 0:TP], RR[:, m, 0:TP], IG[:, m, 0:TP], 0.0, ALU.mult, ALU.add)
            last = V.tensor_tensor_scan(UC[:, m, TP + 3:CW], RR[:, m, TP + 3:CW], IG[:, m, TP + 3:CW],
                                        col(P_H0 + m), ALU.mult, ALU.add)
        chain(last)
        V.tensor_copy(SMALL[:, 48:56].unsqueeze(2), UC[:, :, TP - 1:TP]).then_inc(sem("state_cols"), 1)
        V.tensor_copy(SMALL[:, 56:64].unsqueeze(2), UC[:, :, CW - 1:CW]).then_inc(sem("state_cols"), 1)
        V.tensor_tensor(GT[:, :, 0:TP], GT[:, :, 0:TP], UC[:, :, 0:TP], ALU.mult)
        V.tensor_tensor(GT[:, :, TP:T], GT[:, :, TP:T], UC[:, :, TP + 3:CW], ALU.mult).then_inc(sem("rec"), 1)
        for n, (width, r) in enumerate(((QL, RS[:, :]), (KVL, RELU[:, 0, :]))):
            dve.wait_ge(sem("ssum"), n + 1)
            V.tensor_scalar(r, ps[:, 4 + n, 0:T], D / width, RMS_EPS, ALU.mult, ALU.add).then_inc(sem("rms_eps"), 1)
        for n, r in enumerate((RS[:, :], RELU[:, 0, :])):
            dve.wait_ge(sem("rms_root"), n + 1)
            V.reciprocal(r, r).then_inc(sem("rms"), 1)
        dve.wait_ge(sem("rms"), 2)
        for k in range(4):
            V.scalar_tensor_tensor(out=CQ[:, k, :], in0=CQ[:, k, :], scalar=col(P_QN + k), in1=RS[:, :],
                                   op0=ALU.mult, op1=ALU.mult).then_inc(sem("cq_n"), 1)
        dve.wait_ge(sem("rec_high"), 1)
        sub(XL[:, 0:LT, :], GT[:, :, :], XH[:, 0:LT, :]).then_inc(sem("rec_low"), 1)
        dve.wait_ge(sem("cq_high"), 1)
        sub(CQL[:, :, :], CQ[:, :, :], CQH[:, :, :]).then_inc(sem("cq_low"), 1)
        V.memset(CKT[:, :, KEYS:512], 0.0).then_inc(sem("ck_zero"), 1)
        for k in range(2):
            for src, dst in ((slice(0, TP), slice(0, TP)), (slice(TP, T), slice(TP + PAST, KEYS))):
                V.scalar_tensor_tensor(out=CKT[:, k, dst], in0=CKV[:, k, src], scalar=col(P_KN + k),
                                       in1=RELU[:, 0, src], op0=ALU.mult, op1=ALU.mult).then_inc(sem("ck_n"), 1)
        dve.wait_ge(sem("ck_high"), 1)
        sub(CKL[:, :, :], CKT[:, :, :], CKH[:, :, :]).then_inc(sem("ck_low"), 1)
        split(PHASES["uq"], 0)
        split(PHASES["uq"], 1)
        split(PHASES["uq"], 2)
        split(PHASES["uq"], 3)
        split(PHASES["uq"], 4)
        dve.wait_ge(sem("swap"), 2)
        bc = lambda x, n: x.unsqueeze(1).broadcast_to([P, n, T])
        V.tensor_tensor(SQM[:, :, :], ps[:, 4:8, 0:T], bc(SIN, 4), ALU.mult)
        V.tensor_tensor(RS[:, :], ps[:, 3, 0:T], SIN, ALU.mult)
        V.tensor_tensor(KPE[:, :], KPE[:, :], COS, ALU.mult)
        chain(V.tensor_tensor(QP[:, :, :], QP[:, :, :], bc(COS, 4), ALU.mult))
        V.tensor_tensor(QP[:, :, :], QP[:, :, :], SQM[:, :, :], ALU.add).then_inc(sem("roped_q"), 1)
        V.tensor_tensor(KP[:, 0:TP], KPE[:, 0:TP], RS[:, 0:TP], ALU.add).then_inc(sem("roped"), 1)
        V.tensor_tensor(KP[:, TP + PAST:KEYS], KPE[:, TP:T], RS[:, TP:T], ALU.add).then_inc(sem("roped"), 1)
        split(PHASES["uk"], 1)
        split(PHASES["uv"], 1)

        def maxima(kind, n, x, bank, sm, scale, width, mask):
            dve.wait_ge(*reached(f"{x}_s", n + 1))
            groups = 2 if kind == "p" else 1
            sl = 256 + 8 * (n % 2)
            if groups == 2:
                out, src = sm[:, :], ps[:, bank, :]
                mk = MASK
                v3 = sm[:, :].rearrange("p (t n) -> p t n", t=2)
            else:
                out, src, mk = sm[:, 0:width], ps[:, bank, 0:width], None
                v3 = sm[:, 0:width].unsqueeze(1)
            if mask and groups == 2:
                V.tensor_tensor(out, src, mk, ALU.add).then_inc(sem(f"{x}_sm"), 1)
            else:
                V.tensor_copy(out, src).then_inc(sem(f"{x}_sm"), 1)
            dve.wait_ge(*reached(f"{x}_sm", n + 1))
            chain(V.tensor_reduce(SMALL[:, sl:sl + groups], v3, AX.X, ALU.max))
            V.tensor_scalar(SMALL[:, sl + 2:sl + 2 + groups], SMALL[:, sl:sl + groups], -scale, None, ALU.mult
                            ).then_inc(sem(f"{x}_max"), 1)

        def normalise(kind, n, x, sm, width):
            dve.wait_ge(*reached(f"{x}_exp", n + 1))
            groups = 2 if kind == "p" else 1
            sl = 256 + 8 * (n % 2)
            chain(V.reciprocal(SMALL[:, sl + 6:sl + 6 + groups], SMALL[:, sl + 4:sl + 4 + groups]))
            for t in range(groups):
                last = V.tensor_scalar(sm[:, t * 256:t * 256 + width], sm[:, t * 256:t * 256 + width],
                                       SMALL[:, sl + 6 + t:sl + 7 + t], None, ALU.mult)
            last.then_inc(sem(f"{x}_p"), 1)

        def mla_low(n):
            kind, h = MLA_UNITS[n]
            dve.wait_ge(sem("mla_oh"), n + 1)
            if kind == "p":
                sub(XL[:, LT + h, 0:TP], ps[:, n % 2, 0:TP], XH[:, LT + h, 0:TP]).then_inc(sem("mla_ol"), 1)
            else:
                sub(XL[:, LT + 4 * h:LT + 4 * h + 4, TP:T], ps[:, n % 2, 0:P].rearrange("p (h n) -> p h n", h=4),
                    XH[:, LT + 4 * h:LT + 4 * h + 4, TP:T]).then_inc(sem("mla_ol"), 1)

        NU = len(MLA_UNITS)
        width = lambda n: 256 if MLA_UNITS[n][0] == "p" else PAST + TS

        def mla_max(n):
            if n >= 2:
                dve.wait_ge(sem("mla_t"), n - 1)
            maxima(MLA_UNITS[n][0], n, "mla", 4 + n % 3, SM[n % 2], MLA_SCALE, width(n), True)

        mla_max(0)
        for n in range(NU):
            if n + 1 < NU:
                mla_max(n + 1)
            normalise(MLA_UNITS[n][0], n, "mla", SM[n % 2], width(n))
            if n >= 1:
                mla_low(n - 1)
        mla_low(NU - 1)

        def residual(name, steps, per, blocks_chunks, alpha, post=None):
            c0 = PHASES[name]

            def body(i, last_of_all=False):
                for j in range(per):
                    if not (last_of_all and j == per - 1):
                        split(c0, j + 1, per, i)
                    if j % blocks_chunks == blocks_chunks - 1:
                        b = j // blocks_chunks
                        dve.wait_ge(chunk_used, c0 + j + 1 + per * i)
                        tile = X[:, ds(i * 4 + 2 * b, 2), :]
                        if alpha is not None:
                            ins = V.scalar_tensor_tensor(out=tile, in0=tile, scalar=alpha, in1=ps[:, 2 * b:2 * b + 2, 0:T],
                                                         op0=ALU.mult, op1=ALU.add)
                        else:
                            ins = V.tensor_tensor(tile, tile, ps[:, 2 * b:2 * b + 2, 0:T], ALU.add)
                        ins.then_inc(sem(f"{name}_out{b}"), 1)
            return body

        def residual_phase(name, per, blocks_chunks, alpha, final=False, ln=None):
            if ln:
                dve.wait_ge(*reached(f"{ln}_x", NK))
            body = residual(name, 4, per, blocks_chunks, alpha)
            if final:
                with dve.Fori(0, 3) as i:
                    body(i)
                body(3, True)
            else:
                with dve.Fori(0, 4) as i:
                    body(i)

        def ln(name, l, s, sums, high=True):
            dve.wait_ge(*reached(sums, 1))
            for q in range(4):
                xq = X[:, 4 * q:4 * q + 4, :]
                V.tensor_tensor(xq, xq, ps[:, 4, 0:T].unsqueeze(1).broadcast_to([P, 4, T]), ALU.subtract
                                ).then_inc(sem(f"{name}_d"), 1)
            dve.wait_ge(*reached(f"{name}_var", 1))
            V.tensor_scalar(RS[:, :], ps[:, 5, 0:T], LN_EPS, None, ALU.add).then_inc(sem(f"{name}_eps"), 1)
            dve.wait_ge(*reached(f"{name}_root", 1))
            V.reciprocal(RS[:, :], RS[:, :]).then_inc(sem(f"{name}_rs"), 1)
            dve.wait_ge(*reached(f"{name}_rs", 1))

            def low(q):
                for k in range(4 * q, 4 * q + 4):
                    dve.wait_ge(*reached(f"{name}_high", k + 1))
                    last = V.scalar_tensor_tensor(out=XL[:, k, :], in0=X[:, k, :], scalar=LNB(l, s, k),
                                                  in1=XH[:, k, :].bitcast(f32), op0=ALU.add, op1=ALU.subtract)
                last.then_inc(sem(f"{name}_low"), 1)

            for q in range(4):
                for k in range(4 * q, 4 * q + 4):
                    V.scalar_tensor_tensor(out=X[:, k, :], in0=X[:, k, :], scalar=LNG(l, s, k), in1=RS[:, :],
                                           op0=ALU.mult, op1=ALU.mult).then_inc(sem(f"{name}_t"), 1)
                if high and q >= 1:
                    low(q - 1)
            if high:
                low(3)

        def cross_attention(l):
            x = f"xa{l}"
            with dve.Fori(0, 4) as i:
                for j in range(4):
                    split(PHASES[f"wq{l}"], j + 1, 4, i)

            def mx(n):
                if n >= 2:
                    dve.wait_ge(*reached(f"{x}_t", n - 1))
                if n < 4:
                    maxima("p", n, x, 4 + n % 2, SX[n % 2], XA_SCALE, 256, False)
                else:
                    dve.wait_ge(*reached(f"{x}_s", 4))
                    out = SX[0][:, 0:256]
                    V.tensor_copy(out, ps[:, 6, 0:256]).then_inc(sem(f"{x}_sm"), 1)
                    dve.wait_ge(*reached(f"{x}_sm", 5))
                    chain(V.tensor_reduce(SMALL[:, 256:257], out, AX.X, ALU.max))
                    V.tensor_scalar(SMALL[:, 258:259], SMALL[:, 256:257], -XA_SCALE, None, ALU.mult
                                    ).then_inc(sem(f"{x}_max"), 1)

            def low(n):
                dve.wait_ge(*reached(f"{x}_oh", n + 1))
                if n < 4:
                    sub(XL[:, 4 * n:4 * n + 4, 0:TP], ps[:, 2:4, :].rearrange("p b (m n) -> p (b m) n", m=2),
                        XH[:, 4 * n:4 * n + 4, 0:TP]).then_inc(sem(f"{x}_ol"), 1)
                else:
                    sub(XL[:, :, TP:T], ps[:, 2, :].rearrange("p (m n) -> p m n", m=NK), XH[:, :, TP:T]
                        ).then_inc(sem(f"{x}_ol"), 1)

            mx(0)
            for n in range(5):
                if n + 1 < 5:
                    mx(n + 1)
                normalise("p" if n < 4 else "s", n, x, SX[n % 2], 256)
                low(n)
            residual_phase(f"wo{l}", 4, 2, ALPHA, ln=f"ln{l}0")
            ln(f"ln{l}1", l, 1, f"wo{l}_sum")

        def mlp(l):
            if l == 0:
                dve.wait_ge(sem("stored"), 16 * 8)
            for half, (up, dn) in enumerate((("upa", "downa"), ("upb", "downb"))):
                name = f"{up}{l}"
                c0 = PHASES[name]
                with dve.Fori(0, 8) as i:
                    for j in range(4):
                        split(c0, j + 1, 4, i)
                        if j % 2 == 1:
                            b = j // 2
                            dve.wait_ge(*reached(f"{name}_high{b}", i + 1))
                            t = ds(i * 4 + 2 * b, 2)
                            sub(HL[:, t, :], SQH[:, b, :, :], HH[:, t, :]).then_inc(sem(f"{name}_low{b}"), 1)
                residual_phase(f"{dn}{l}", 8, 4, ALPHA if half == 0 else None, final=half == 1 and l == 1, ln=f"ln{l}1")
            ln(f"ln{l}2", l, 2, f"downb{l}_sum", high=False)

        residual_phase("wout", 4, 2, ALPHA)
        ln("ln00", 0, 0, "wout_sum")
        cross_attention(0)
        mlp(0)
        dve.wait_ge(sem("ext"), 4)
        dve.wait_ge(sem("poolT_out"), 1)
        levels = ((EXT, 0, S2, 0, 1), (S2, 4, S4, 4, 2), (S4, 8, S8, 8, 4), (S8, 12, S16, 12, 8))
        offs = {id(EXT): 0, id(S2): 0, id(S4): 4, id(S8): 8, id(S16): 12}
        for src, _, dst, k0, sh in levels:
            n = NK - k0
            so, do = k0 - offs[id(src)], k0 - offs[id(dst)]
            w0 = 2 * sh - 1
            ins = V.tensor_tensor(dst[:, do:do + n, w0:EW], src[:, so:so + n, w0:EW],
                                  src[:, so:so + n, w0 - sh:EW - sh], ALU.add)
            chain(ins)
        split(PHASES["pool"], 1)
        for g, (src, w) in enumerate(zip((S2, S4, S8, S16), WINDOWS)):
            so = 4 * g - offs[id(src)]
            e = EXT[:, 4 * g:4 * g + 4, :]
            win_ = src[:, so:so + 4, :]
            diff = SQH[:, :, :, :].rearrange("p a b n -> p (a b) n")
            head = SMALL[:, 272:336].rearrange("p (k n) -> p k n", k=4)
            a0, c0 = PBUF, 2 * PBUF + TP
            cnt = CST[:, C_CNT + 16 * g:C_CNT + 16 * g + 16].unsqueeze(1).broadcast_to([P, 4, 16])
            chain(V.tensor_tensor(head, win_[:, :, a0:a0 + 16], cnt, ALU.mult))
            V.tensor_tensor(diff[:, :, 0:16], head, e[:, :, a0:a0 + 16], ALU.subtract)
            V.scalar_tensor_tensor(out=diff[:, :, 16:TP], in0=win_[:, :, a0 + 16:a0 + TP], scalar=1.0 / w,
                                   in1=e[:, :, a0 + 16:a0 + TP], op0=ALU.mult, op1=ALU.subtract)
            V.scalar_tensor_tensor(out=diff[:, :, TP:T], in0=win_[:, :, c0:c0 + TS], scalar=1.0 / w,
                                   in1=e[:, :, c0:c0 + TS], op0=ALU.mult, op1=ALU.subtract
                                   ).then_inc(sem("pool_d"), 1)
            dve.wait_ge(sem("pool_high"), g + 1)
            sub(XL[:, 4 * g:4 * g + 4, :], diff, XH[:, 4 * g:4 * g + 4, :]).then_inc(sem("pool_low"), 1)
        for g in range(4):
            if g:
                split(PHASES["pool"], g + 1)
            for m in range(4):
                n = 4 * g + m
                dve.wait_ge(sem("pool_y"), n + 1)
                V.scalar_tensor_tensor(out=X[:, n, :], in0=X[:, n, :], scalar=ALPHA, in1=RELU[:, n % 2, :],
                                       op0=ALU.mult, op1=ALU.add).then_inc(sem("pool_x"), 1)
        ln("ln10", 1, 0, "pool_sum")
        cross_attention(1)
        mlp(1)

    stack.close()


def constants():
    c = np.zeros((P, C_END), np.float32)
    c[:, C_ID:C_ID + P] = np.eye(P, dtype=np.float32)
    r = np.arange(P)
    c[r, C_PERM + (r ^ 32)] = 1.0
    half = ROPE // 2
    inv = (np.float32(10000.0) ** (-np.arange(half, dtype=np.float32) / half)).astype(np.float32)
    pos = np.concatenate([np.arange(TP), PAST + np.arange(TS)]).astype(np.float32)
    ang = (pos[None, :] * inv[:, None]).astype(np.float32)
    cos, sin = np.cos(ang), np.sin(ang)
    c[:, C_COS:C_COS + T] = np.tile(cos, (4, 1))
    c[:, C_SIN:C_SIN + T] = np.tile(np.concatenate([-sin, sin]), (2, 1))
    q = np.arange(TP).reshape(2, P)
    k = np.arange(TP)
    mask = np.where(k[None, None, :] // 64 <= q[:, :, None] // 64, 0.0, -1e30).astype(np.float32)
    c[:, C_MASK:C_MASK + 512] = mask.transpose(1, 0, 2).reshape(P, 512)
    for g, w in enumerate(WINDOWS):
        c[:, C_CNT + 16 * g:C_CNT + 16 * g + 16] = (1.0 / np.minimum(np.arange(16) + 1, w)).astype(np.float32)
    return c


INS = ["x_prompt", "x_sample", "mem_prompt", "cache_mem_k", "cache_mem_v", "cache_mla_ckv", "cache_mla_kpe",
       "state_rglru_h", "state_rglru_conv", "state_pool", "w_in", "q_norm_g", "w_uq", "kv_norm_g", "w_uk", "w_uv",
       "conv_w", "conv_b", "gate_a_w", "gate_a_b", "gate_x_w", "gate_x_b", "lru_lambda", "w_out", "pool_w",
       "pool_scale", "xa_wq", "xa_wk", "xa_wv", "xa_wo", "mlp_up", "mlp_down", "ln_g", "ln_b"]
OUTS = [("y_prompt", (1, TP, D)), ("y_sample", (1, TS, D)), ("p_conv", (1, 1, 3, LW)), ("p_h", (1, 1, LW)),
        ("p_ckv", (1, 1, TP, KVL)), ("p_kpe", (1, 1, TP, ROPE)), ("p_pool", (1, 1, PBUF, D)),
        ("p_mem_k", (2, 1, NMEM, D)), ("p_mem_v", (2, 1, NMEM, D)), ("s_conv", (1, 1, 3, LW)), ("s_h", (1, 1, LW)),
        ("s_ckv", (1, 1, TS, KVL)), ("s_kpe", (1, 1, TS, ROPE)), ("s_pool", (1, 1, PBUF, D))]


def kernel(**inputs):
    import concourse.bacc as bacc
    from concourse.bass_utils import run_bass_kernel_spmd

    nc = bacc.Bacc("TRN2", target_bir_lowering=False, num_devices=1)
    arrays = {f"in_{n}": np.ascontiguousarray(inputs[n]) for n in INS}
    arrays["in_cst"] = constants()
    a = {n[3:]: nc.dram_tensor(n, x.shape, mybir.dt.from_np(x.dtype), kind="ExternalInput").ap()
         for n, x in arrays.items()}
    o = {n: nc.dram_tensor(f"out_{n}", s, mybir.dt.float32, kind="ExternalOutput").ap() for n, s in OUTS}
    build(nc, a, o)
    r = run_bass_kernel_spmd(nc, [arrays], core_ids=[0])
    return tuple(r.results[0][f"out_{n}"] for n, _ in OUTS)
```
